# Optimizing a Trainium2 kernel written in Bass

```python
import jax, jax.numpy as jnp
from jax import lax
import numpy as np
import math

D_MODEL = 1024
BATCH = 1
SEQ = 512
DEPTH = 2

N_CONV_LAYERS = DEPTH // 2
N_ATTN_LAYERS = DEPTH - N_CONV_LAYERS
CONV_WIDTH = 3
HEAD_DIM = 64
N_HEADS = D_MODEL // HEAD_DIM
BRANCHES = ((128, 1), (512, 4), (2048, 16))
N_BRANCHES = len(BRANCHES)
Q_WIDTH = N_BRANCHES * N_HEADS * HEAD_DIM
D_FF = -(-8 * D_MODEL // (3 * 256)) * 256
ROPE_THETA = 10000.0
RMS_EPS = 1e-6
NEG_INF = -1e30


def rms_norm(x, g):
    xf = x.astype(jnp.float32)
    y = xf * lax.rsqrt(jnp.mean(xf * xf, axis=-1, keepdims=True) + RMS_EPS)
    return (y * g.astype(jnp.float32)).astype(x.dtype)

def rope(t, positions):
    half = HEAD_DIM // 2
    inv_freq = ROPE_THETA ** (-jnp.arange(half, dtype=jnp.float32) / half)
    ang = positions.astype(jnp.float32)[..., None] * inv_freq
    cos = jnp.cos(ang)[:, :, None, :]
    sin = jnp.sin(ang)[:, :, None, :]
    t1 = t[..., :half].astype(jnp.float32)
    t2 = t[..., half:].astype(jnp.float32)
    out = jnp.concatenate([t1 * cos - t2 * sin, t2 * cos + t1 * sin], axis=-1)
    return out.astype(t.dtype)

def short_conv_mixer(x, w_in, conv_w, w_out):
    b_gate, c_gate, h = jnp.split(x @ w_in, 3, axis=-1)
    u = c_gate * h
    rhs = conv_w[:, None, :].astype(u.dtype)
    conv = lax.conv_general_dilated(
        u, rhs, window_strides=(1,), padding=[(CONV_WIDTH - 1, 0)],
        dimension_numbers=("NWC", "WIO", "NWC"), feature_group_count=u.shape[-1])
    return (b_gate * conv) @ w_out

def swiglu(x, w_gate_up, w_down):
    g, u = jnp.split(x @ w_gate_up, 2, axis=-1)
    return (jax.nn.silu(g) * u) @ w_down

def dilated_branch(q, k, v, window, dilation):
    band = window // dilation
    B, S, H, Dh = q.shape
    chunk = dilation * band
    Sp = -(-S // chunk) * chunk
    nb = Sp // chunk
    pad = ((0, 0), (0, Sp - S), (0, 0), (0, 0))

    def to_blocks(t):
        t = jnp.pad(t, pad).reshape(B, nb, band, dilation, H, Dh)
        return t.transpose(0, 3, 4, 1, 2, 5)

    def with_prev(t):
        prev = jnp.pad(t, ((0, 0), (0, 0), (0, 0), (1, 0), (0, 0), (0, 0)))[:, :, :, :-1]
        return jnp.concatenate([prev, t], axis=4)

    qb = to_blocks(q * (HEAD_DIM ** -0.5))
    kk = with_prev(to_blocks(k))
    vv = with_prev(to_blocks(v))
    s = jnp.einsum("brhnqd,brhnkd->brhnqk", qb, kk).astype(jnp.float32)
    qi = jnp.arange(band)[:, None]
    kj = jnp.arange(2 * band)[None, :]
    dist = qi + band - kj
    in_band = (dist >= 0) & (dist <= band)
    has_prev = (kj >= band)[None] | (jnp.arange(nb)[:, None, None] > 0)
    mask = in_band[None] & has_prev
    s = jnp.where(mask, s, NEG_INF)
    m = jnp.max(s, axis=-1)
    p = jnp.exp(s - m[..., None])
    l = jnp.sum(p, axis=-1)
    o = jnp.einsum("brhnqk,brhnkd->brhnqd", p, vv.astype(jnp.float32)) / l[..., None]
    lse = m + jnp.log(l)
    o = o.transpose(0, 3, 4, 1, 2, 5).reshape(B, Sp, H, Dh)[:, :S]
    lse = lse.transpose(0, 3, 4, 1, 2).reshape(B, Sp, H)[:, :S]
    return o, lse

def dilated_attention_mixer(x, positions, k_sh, v_sh, w_q, w_o):
    B, S, _ = x.shape
    q = (x @ w_q).reshape(B, S, N_BRANCHES * N_HEADS, HEAD_DIM)
    q = rope(q, positions).reshape(B, S, N_BRANCHES, N_HEADS, HEAD_DIM)
    outs, lses = [], []
    for g, (window, dilation) in enumerate(BRANCHES):
        o, lse = dilated_branch(q[:, :, g], k_sh[:, :, g], v_sh[:, :, g], window, dilation)
        outs.append(o)
        lses.append(lse)
    wts = jax.nn.softmax(jnp.stack(lses, axis=0), axis=0)
    o = jnp.einsum("gbsh,gbshd->bshd", wts, jnp.stack(outs, axis=0))
    return o.astype(x.dtype).reshape(B, S, N_HEADS * HEAD_DIM) @ w_o

def shared_kv(h, positions, kv_norm, w_kv):
    B, S, _ = h.shape
    kv = (rms_norm(h, kv_norm) @ w_kv).reshape(B, S, 2, N_BRANCHES * N_HEADS, HEAD_DIM)
    k = rope(kv[:, :, 0], positions).reshape(B, S, N_BRANCHES, N_HEADS, HEAD_DIM)
    v = kv[:, :, 1].reshape(B, S, N_BRANCHES, N_HEADS, HEAD_DIM)
    return k, v

def first_inputs(seed: int = 0) -> dict:
    key = jax.random.key(seed)
    ks = jax.random.split(key, 20)
    f32 = jnp.float32

    def w(k, shape, fan_in):
        return jax.random.normal(k, shape, f32) * (fan_in ** -0.5)

    def gain(k, shape):
        return 1.0 + 0.05 * jax.random.normal(k, shape, f32)

    x = jax.random.normal(ks[0], (BATCH, SEQ, D_MODEL), f32)
    offset = jax.random.randint(ks[1], (BATCH, 1), 0, 4096, dtype=jnp.int32)
    positions = offset + jnp.arange(SEQ, dtype=jnp.int32)[None, :]
    nA, nB = N_CONV_LAYERS, N_ATTN_LAYERS
    return {
        "x": x,
        "positions": positions,
        "mix_norm_pre": gain(ks[2], (DEPTH, D_MODEL)),
        "mix_norm_post": gain(ks[3], (DEPTH, D_MODEL)),
        "ffn_norm_pre": gain(ks[4], (DEPTH, D_MODEL)),
        "ffn_norm_post": gain(ks[5], (DEPTH, D_MODEL)),
        "ffn_w_gate_up": w(ks[6], (DEPTH, D_MODEL, 2 * D_FF), D_MODEL),
        "ffn_w_down": w(ks[7], (DEPTH, D_FF, D_MODEL), D_FF),
        "conv_w_in": w(ks[8], (nA, D_MODEL, 3 * D_MODEL), D_MODEL),
        "conv_w": w(ks[9], (nA, CONV_WIDTH, D_MODEL), CONV_WIDTH),
        "conv_w_out": w(ks[10], (nA, D_MODEL, D_MODEL), D_MODEL),
        "kv_norm": gain(ks[11], (D_MODEL,)),
        "w_kv": w(ks[12], (D_MODEL, 2 * Q_WIDTH), D_MODEL),
        "w_q": w(ks[13], (nB, D_MODEL, Q_WIDTH), D_MODEL),
        "w_o": w(ks[14], (nB, N_HEADS * HEAD_DIM, D_MODEL), N_HEADS * HEAD_DIM),
    }

def first_block(x, positions, mix_norm_pre, mix_norm_post, ffn_norm_pre, ffn_norm_post,
              ffn_w_gate_up, ffn_w_down, conv_w_in, conv_w, conv_w_out,
              kv_norm, w_kv, w_q, w_o):
    h = x
    for layer in range(DEPTH):
        if layer == N_CONV_LAYERS:
            k_sh, v_sh = shared_kv(h, positions, kv_norm, w_kv)
        hn = rms_norm(h, mix_norm_pre[layer])
        if layer < N_CONV_LAYERS:
            y = short_conv_mixer(hn, conv_w_in[layer], conv_w[layer], conv_w_out[layer])
        else:
            j = layer - N_CONV_LAYERS
            y = dilated_attention_mixer(hn, positions, k_sh, v_sh, w_q[j], w_o[j])
        h = h + rms_norm(y, mix_norm_post[layer])
        f = swiglu(rms_norm(h, ffn_norm_pre[layer]), ffn_w_gate_up[layer], ffn_w_down[layer])
        h = h + rms_norm(f, ffn_norm_post[layer])
    return h


DEPTH_2 = 1

D_MIX = D_MODEL
N_Q_HEADS = 8
N_KV_HEADS = 2
Q_PER_KV = N_Q_HEADS // N_KV_HEADS
D_ATTN = N_Q_HEADS * HEAD_DIM
D_CONV = D_MIX - D_ATTN
CONV_WIDTH_2 = 31
WINDOW = 128
BLOCK = 128
N_BUCKETS = 32
MAX_EXACT = N_BUCKETS // 2
MAX_DISTANCE = 128
D_FF_2 = int(math.ceil(8 * D_MODEL / 3 / 256) * 256)
EPS = 1e-6
D_Q = N_Q_HEADS * HEAD_DIM
D_KV = N_KV_HEADS * HEAD_DIM
D_IN = D_Q + 2 * D_KV + 2 * D_CONV


def rms_norm_2(x, g):
    xf = x.astype(jnp.float32)
    y = xf * lax.rsqrt(jnp.mean(xf * xf, axis=-1, keepdims=True) + EPS)
    return (y * g.astype(jnp.float32)).astype(x.dtype)

def layer_norm(x, g, b):
    xf = x.astype(jnp.float32)
    mu = jnp.mean(xf, axis=-1, keepdims=True)
    var = jnp.mean(jnp.square(xf - mu), axis=-1, keepdims=True)
    y = (xf - mu) * lax.rsqrt(var + EPS)
    return (y * g.astype(jnp.float32) + b.astype(jnp.float32)).astype(x.dtype)

def t5_causal_bucket(dist):
    is_small = dist < MAX_EXACT
    d = jnp.maximum(dist, 1).astype(jnp.float32)
    large = MAX_EXACT + (jnp.log(d / MAX_EXACT) / math.log(MAX_DISTANCE / MAX_EXACT)
                         * (N_BUCKETS - MAX_EXACT)).astype(jnp.int32)
    large = jnp.minimum(large, N_BUCKETS - 1)
    return jnp.where(is_small, dist, large)

def conformer_conv(u, conv_dw, conv_dw_b, conv_ln_g, conv_ln_b, w_conv_pw):
    a, gate = jnp.split(u, 2, axis=-1)
    h = a * jax.nn.sigmoid(gate)
    h = lax.conv_general_dilated(
        h, conv_dw[:, None, :].astype(h.dtype), window_strides=(1,),
        padding=[(CONV_WIDTH_2 - 1, 0)],
        dimension_numbers=("NWC", "WIO", "NWC"),
        feature_group_count=D_CONV) + conv_dw_b
    h = jax.nn.silu(layer_norm(h, conv_ln_g, conv_ln_b))
    return h @ w_conv_pw

def sliding_window_attention(q, k, v, attn_sinks, rel_bias):
    B, S = q.shape[0], q.shape[1]
    nb = S // BLOCK
    qb = q.reshape(B, nb, BLOCK, N_KV_HEADS, Q_PER_KV, HEAD_DIM)
    pad = ((0, 0), (BLOCK, 0), (0, 0), (0, 0))
    kp, vp = jnp.pad(k, pad), jnp.pad(v, pad)

    def band(t):
        prev = t[:, :S].reshape(B, nb, BLOCK, N_KV_HEADS, HEAD_DIM)
        cur = t[:, BLOCK:].reshape(B, nb, BLOCK, N_KV_HEADS, HEAD_DIM)
        return jnp.concatenate([prev, cur], axis=2)

    kb, vb = band(kp), band(vp)
    scale = 1.0 / math.sqrt(HEAD_DIM)
    s = jnp.einsum("bnqhgd,bnkhd->bnhgqk", qb, kb).astype(jnp.float32) * scale

    qi = jnp.arange(BLOCK)[:, None]
    kj = jnp.arange(2 * BLOCK)[None, :]
    dist = qi + BLOCK - kj
    in_band = (dist >= 0) & (dist < WINDOW)
    bucket = t5_causal_bucket(jnp.maximum(dist, 0))
    bias = rel_bias.astype(jnp.float32)[bucket]
    bias = jnp.transpose(bias, (2, 0, 1)).reshape(N_KV_HEADS, Q_PER_KV, BLOCK, 2 * BLOCK)
    blk = jnp.arange(nb)[:, None, None]
    valid = in_band[None] & ((blk > 0) | (kj[None] >= BLOCK))
    s = jnp.where(valid[None, :, None, None], s + bias, -jnp.inf)

    sink = attn_sinks.astype(jnp.float32).reshape(N_KV_HEADS, Q_PER_KV, 1, 1)
    m = jnp.maximum(jnp.max(s, axis=-1, keepdims=True), sink)
    p = jnp.exp(s - m)
    denom = jnp.sum(p, axis=-1, keepdims=True) + jnp.exp(sink - m)
    p = (p / denom).astype(v.dtype)
    o = jnp.einsum("bnhgqk,bnkhd->bnqhgd", p, vb)
    return o.reshape(B, S, N_Q_HEADS * HEAD_DIM)

def second_inputs(seed: int = 0) -> dict:
    key = jax.random.key(seed)
    ks = jax.random.split(key, 20)
    f = jnp.float32
    nrm = lambda k, shp, sc: jax.random.normal(k, shp, f) * sc
    gain = lambda k, n: 1.0 + 0.05 * jax.random.normal(k, (n,), f)
    return {
        "x": jax.random.normal(ks[0], (BATCH, SEQ, D_MODEL), f),
        "mix_pre_g": gain(ks[1], D_MODEL),
        "mix_post_g": gain(ks[2], D_MODEL),
        "ffn_pre_g": gain(ks[3], D_MODEL),
        "ffn_post_g": gain(ks[4], D_MODEL),
        "w_in": nrm(ks[5], (D_MODEL, D_IN), D_MODEL ** -0.5),
        "conv_dw": nrm(ks[6], (CONV_WIDTH_2, D_CONV), CONV_WIDTH_2 ** -0.5),
        "conv_dw_b": nrm(ks[7], (D_CONV,), 0.02),
        "conv_ln_g": gain(ks[8], D_CONV),
        "conv_ln_b": nrm(ks[9], (D_CONV,), 0.02),
        "w_conv_pw": nrm(ks[10], (D_CONV, D_CONV), D_CONV ** -0.5),
        "attn_sinks": nrm(ks[11], (N_Q_HEADS,), 0.5),
        "rel_bias": nrm(ks[12], (N_BUCKETS, N_Q_HEADS), 0.5),
        "w_out": nrm(ks[13], (D_MIX, D_MODEL), D_MIX ** -0.5),
        "w_gate": nrm(ks[14], (D_MODEL, D_FF_2), D_MODEL ** -0.5),
        "w_up": nrm(ks[15], (D_MODEL, D_FF_2), D_MODEL ** -0.5),
        "w_down": nrm(ks[16], (D_FF_2, D_MODEL), D_FF_2 ** -0.5),
    }

def second_block(x, mix_pre_g, mix_post_g, ffn_pre_g, ffn_post_g, w_in, conv_dw, conv_dw_b,
              conv_ln_g, conv_ln_b, w_conv_pw, attn_sinks, rel_bias, w_out,
              w_gate, w_up, w_down):
    B, S, _ = x.shape
    h = x
    for _layer in range(DEPTH_2):
        hn = rms_norm_2(h, mix_pre_g)
        proj = hn @ w_in
        q = proj[..., :D_Q].reshape(B, S, N_Q_HEADS, HEAD_DIM)
        k = proj[..., D_Q:D_Q + D_KV].reshape(B, S, N_KV_HEADS, HEAD_DIM)
        v = proj[..., D_Q + D_KV:D_Q + 2 * D_KV].reshape(B, S, N_KV_HEADS, HEAD_DIM)
        u = proj[..., D_Q + 2 * D_KV:]
        attn_out = sliding_window_attention(q, k, v, attn_sinks, rel_bias)
        conv_out = conformer_conv(u, conv_dw, conv_dw_b, conv_ln_g, conv_ln_b, w_conv_pw)
        mixed = jnp.concatenate([attn_out, conv_out], axis=-1) @ w_out
        h = h + rms_norm_2(mixed, mix_post_g)
        hn = rms_norm_2(h, ffn_pre_g)
        ff = (jax.nn.silu(hn @ w_gate) * (hn @ w_up)) @ w_down
        h = h + rms_norm_2(ff, ffn_post_g)
    return h


def setup_inputs(seed=0):
    out = dict(first_inputs(seed))
    for name, value in second_inputs(seed + 1).items():
        if name != "x":
            out[name + "_2"] = value
    return out


def reference(
    x, positions, mix_norm_pre, mix_norm_post, ffn_norm_pre, ffn_norm_post, ffn_w_gate_up,
    ffn_w_down, conv_w_in, conv_w, conv_w_out, kv_norm, w_kv, w_q, w_o, mix_pre_g_2,
    mix_post_g_2, ffn_pre_g_2, ffn_post_g_2, w_in_2, conv_dw_2, conv_dw_b_2, conv_ln_g_2,
    conv_ln_b_2, w_conv_pw_2, attn_sinks_2, rel_bias_2, w_out_2, w_gate_2, w_up_2, w_down_2,
):
    x = first_block(
        x, positions, mix_norm_pre, mix_norm_post, ffn_norm_pre, ffn_norm_post, ffn_w_gate_up,
        ffn_w_down, conv_w_in, conv_w, conv_w_out, kv_norm, w_kv, w_q, w_o,
    )
    return second_block(
        x, mix_pre_g_2, mix_post_g_2, ffn_pre_g_2, ffn_post_g_2, w_in_2, conv_dw_2, conv_dw_b_2,
        conv_ln_g_2, conv_ln_b_2, w_conv_pw_2, attn_sinks_2, rel_bias_2, w_out_2, w_gate_2,
        w_up_2, w_down_2,
    )


_drawn_inputs = setup_inputs


def setup_inputs(seed=0):
    import zlib

    import numpy as np

    out = dict(_drawn_inputs(seed))
    spreads = {}
    factors = {'ffn_post_g_2': 3.055, 'conv_dw_b_2': 3.68, 'conv_ln_b_2': 7.568, 'attn_sinks_2': 8.0}
    for name, (base, spread) in spreads.items():
        noise = np.random.default_rng([zlib.crc32(name.encode()), seed]).standard_normal(out[name].shape)
        drawn = base * np.exp(spread * noise) if base else spread * noise
        out[name] = __import__('jax').numpy.asarray(drawn.astype(out[name].dtype))
    for name, factor in factors.items():
        out[name] = (out[name] * factor).astype(out[name].dtype)
    return out
```

```python
import math
from contextlib import ExitStack

import numpy as np

import concourse.bass as bass
from concourse import mybir

F32 = mybir.dt.float32
F32R = mybir.dt.float32r
BF16 = mybir.dt.bfloat16
I32 = mybir.dt.int32
ACT = mybir.ActivationFunctionType
ALU = mybir.AluOpType
AX = mybir.AxisListType

P = 128
S = 512
D = 1024
KC = D // P
D_FF = 2816
FC = D_FF // P
HD = 64
HALF = HD // 2
EPS = 1e-6
NEG = -1e30
TAPS1 = 3
TAPS2 = 31
C2 = 512
CB = C2 // P
UNIT = 2048

CONV_IN = 0
CONV_OUT = CONV_IN + 12
FFN_A = CONV_OUT + 4
DOWN_A = FFN_A + FC
QKV = DOWN_A + FC // 2
ATT_OUT = QKV + 36
FFN_B = ATT_OUT + 4
DOWN_B = FFN_B + FC
IN2 = DOWN_B + FC // 2
PW2 = IN2 + 7
OUT2 = PW2 + 1
FFN_C = OUT2 + 4
DOWN_C = FFN_C + FC
UNITS = DOWN_C + FC // 2

EV_CONV, EV_FFN_A = 0, 12
EV_QKV = EV_FFN_A + FC
EV_FFN_B = EV_QKV + 36
EV_IN2 = EV_FFN_B + FC
EV_FFN_C = EV_IN2 + 7

G_MIX_PRE, G_MIX_POST, G_FFN_PRE, G_FFN_POST = 0, 16, 32, 48
G_KV = 64
G2_MIX_PRE, G2_MIX_POST, G2_FFN_PRE, G2_FFN_POST = 72, 80, 88, 96
CONVW = 104
INV_FREQ = CONVW + TAPS1 * KC
PCOLS = INV_FREQ + 1
CDW = 0
CDB = CDW + TAPS2 * CB
LNG = CDB + CB
LNB = LNG + CB
SINK = LNB + CB
P2COLS = SINK + 8

POST_GAIN = [None, G_MIX_POST, G_FFN_POST, G_MIX_POST + KC, G_FFN_POST + KC, G2_MIX_POST, G2_FFN_POST]
X_COUNT = [1, 1, 2, 1, 1, 1, 0]
X_BASE = [KC * sum(X_COUNT[:t]) for t in range(8)]
LAST_ROWS = [None, FFN_A - 1, QKV - 1, FFN_B - 1, IN2 - 1, FFN_C - 1, UNITS - 1]

PI_CLAMP = 3.1415925
TWO_PI_1, TWO_PI_2, TWO_PI_3 = 6.28125, 1.9350051879882812e-3, 3.0199159819567528e-7


class SelfOrder:

    def __init__(self, eng, sem):
        self.eng, self.sem, self.n, self.i, self.per = eng, sem, 0, None, 0

    def mark(self, ins):
        ins.then_inc(self.sem, 1)
        self.n += 1

    def value(self, back=0):
        v = self.n - back
        return v if self.i is None else self.per * self.i + v

    def wait(self, back=0):
        self.eng.wait_ge(self.sem, self.value(back))

    def link(self, ins):
        self.mark(ins)
        self.wait()

    def enter(self, i, per):
        self.i, self.per, self.start = i, per, self.n

    def leave(self, turns):
        assert self.n - self.start == self.per, (self.n - self.start, self.per)
        self.i = None
        self.n = self.start + self.per * turns


def run(i, per, v):
    return v if i is None else per * i + v


def program(nc, x_t, pos, w_all, par, par2, masks, ident_c, zr_c, rel, onehot, skew, out_t):
    ctx = ExitStack()
    with ctx:
        cursor = [-(-nc.sbuf_base // 32) * 32]

        def sb(name, shape, dt=F32, at=None):
            size = int(np.prod(shape[1:])) * (2 if dt == BF16 else 4)
            if at is None:
                at = cursor[0]
                cursor[0] += -(-size // 32) * 32
            assert at + size <= nc.sbuf_usable_end, (name, at + size)
            return nc.alloc_sbuf_tensor_at(name, shape, dt, offset=at)

        def sem(name):
            return ctx.enter_context(nc.semaphore(name))

        h = sb("h", [P, KC, S])
        w_raw = [sb(f"w_raw{p}", [P, UNIT]) for p in range(2)]
        w_hi = [sb(f"w_hi{p}", [P, UNIT], F32R) for p in range(2)]
        w_lo = [sb(f"w_lo{p}", [P, UNIT], F32R) for p in range(2)]
        x_hi = sb("x_hi", [P, KC, S], F32R)
        x_lo = sb("x_lo", [P, KC, S], F32R)
        region = cursor[0]
        ff_hi = sb("ff_hi", [P, FC, S], F32R)
        ff_lo = sb("ff_lo", [P, FC, S], F32R)
        cursor[0] += 2048
        K16 = KC * S * 4
        y = sb("y", [P, KC, S], at=region)
        mix_hi = sb("mix_hi", [P, KC, S], F32R, at=region + K16)
        mix_lo = sb("mix_lo", [P, KC, S], F32R, at=region + 2 * K16)
        tail = region + 3 * K16
        u1 = sb("u1", [P, 2, S + 2], at=tail)
        cg = sb("cg", [P, 2, S], at=tail + 4160)
        cv = sb("cv", [P, 2, S], at=tail + 4160 + 4096)
        o_t = sb("o_t", [P, KC, S], at=region)
        qk = sb("qk", [P, 12, S], at=tail)
        v_at = tail + 12 * S * 4
        v1s = [sb(f"v1s{b}", [P, 4, 2, 3 * HD], at=v_at + b * 4 * 2 * 3 * HD * 4) for b in range(3)]
        t2 = sb("t2", [P, 8, 256], at=region)
        p2 = sb("p2", [P, 8, 256], at=region + 8192)
        q2 = sb("q2", [P, 4, S], at=tail)
        k2 = sb("k2", [P, S], at=tail + 8192)
        v2 = sb("v2", [P, 4, P], at=tail + 8192 + 2048)
        u2_at = tail + 8192 + 4096
        u2 = sb("u2", [P, CB, S + 32], at=u2_at)
        c2_at = u2_at + CB * (S + 32) * 4
        c2 = sb("c2", [P, CB, S], at=c2_at)
        bias2 = sb("bias2", [P, 8, 256], at=c2_at + CB * S * 4)
        par2_s = sb("par2_s", [P, P2COLS], at=c2_at + CB * S * 4 + 8192)
        work_at = cursor[0]
        work = sb("work", [P, 6, S])
        r_pre = sb("r_pre", [P, S])
        cos_t = sb("cos_t", [P, S])
        sin_t = sb("sin_t", [P, S])
        par_s = sb("par_s", [P, PCOLS])
        mask_b = sb("mask_b", [P, 3 * P], BF16)
        ident = sb("ident", [P, P])
        ident_b = sb("ident_b", [P, P], BF16)
        zr = sb("zr", [P, P + 3])
        ones = sb("ones", [P, P])
        eps_t = sb("eps_t", [P, 1])
        r_col = sb("r_col", [P, 8])
        st = sb("st", [P, 96])
        ACC, TMP, RQ = 0, 3, 5
        p0 = sb("p0", [P, 2, 4, 256], at=work_at)
        pq = sb("pq", [P, 2, 256], at=4 * S * 4 + work_at)
        pt = sb("pt", [P, 2, 256], at=5 * S * 4 + work_at)
        ln_l = sb("ln_l", [P, 2, S], at=work_at)
        pt2 = sb("pt2", [P, 4, S], at=work_at)
        nm0, nm0r, nm, c0, c0n, cm, cdiff = (st[:, 0:8], st[:, 8:16], st[:, 16:24], st[:, 24:32],
                                      st[:, 32:40], st[:, 40:72], st[:, 72:80])
        nm2, nsink, l2, es2, rl2 = st[:, 0:8], st[:, 8:16], st[:, 16:24], st[:, 24:32], st[:, 32:40]
        rel_s = sb("rel_s", [P, 8], at=tail)
        onehot_s = sb("onehot_s", [P, 384], at=tail + 64)
        erow = sb("erow", [P, 384], at=tail + 2048)
        pos_i = sb("pos_i", [P, S], I32, at=tail + 4096)
        ang = sb("ang", [P, S], at=tail + 6144)
        turn = sb("turn", [P, S], I32, at=tail + 8192)
        mask_f = sb("mask_f", [P, 3 * P], at=tail + 10240)

        bank = [ctx.enter_context(nc.psum_tensor(f"bank{i}", [P, S], F32)) for i in range(8)]

        w_landed = [sem(f"w_landed{p}") for p in range(2)]
        w_rounded = sem("w_rounded")
        w_split = sem("w_split")
        unit_done = sem("unit_done")
        evac = sem("evac")
        h_loaded = sem("h_loaded")
        par_loaded = sem("par_loaded")
        par2_loaded = sem("par2_loaded")
        skew_written = sem("skew_written")
        bias_loaded = sem("bias_loaded")
        out_written = sem("out_written")
        consts_ready = sem("consts_ready")
        casts_ready = sem("casts_ready")
        y_done = sem("y_done")
        y_copied = sem("y_copied")
        ysq_done = sem("ysq_done")
        yacc_done = sem("yacc_done")
        ystat_done = sem("ystat_done")
        yr_ready = sem("yr_ready")
        h_ready = sem("h_ready")
        xhi_done = sem("xhi_done")
        x_ready = sem("x_ready")
        xsq_done = sem("xsq_done")
        xacc_done = sem("xacc_done")
        xstat_done = sem("xstat_done")
        xr_ready = sem("xr_ready")
        mixf_ready = sem("mixf_ready")
        mixhi_done = sem("mixhi_done")
        mix_ready = sem("mix_ready")
        silu_done = sem("silu_done")
        fff_ready = sem("fff_ready")
        ffhi_done = sem("ffhi_done")
        ff_ready = sem("ff_ready")
        angle_ready = sem("angle_ready")
        trig_done = sem("trig_done")
        rcol_ps = sem("rcol_ps")
        rcol_ready = sem("rcol_ready")
        at_scores = sem("at_scores")
        at_negmax = sem("at_negmax")
        at_exp = sem("at_exp")
        at_perm = sem("at_perm")
        at_diff = sem("at_diff")
        at_c0 = sem("at_c0")
        at_cm = sem("at_cm")
        at_scaled = sem("at_scaled")
        at_trans = sem("at_trans")
        at_ptcopy = sem("at_ptcopy")
        at_av = sem("at_av")
        at_rl = sem("at_rl")
        at_out = sem("at_out")
        b_row = sem("b_row")
        b_rowcopied = sem("b_rowcopied")
        b_scores = sem("b_scores")
        b_logits = sem("b_logits")
        b_negmax = sem("b_negmax")
        b_exp = sem("b_exp")
        b_prob = sem("b_prob")
        b_trans = sem("b_trans")
        b_ptcopy = sem("b_ptcopy")
        b_av = sem("b_av")
        sig_done = sem("sig_done")
        conv_ready = sem("conv_ready")
        ln_sum = sem("ln_sum")
        ln_mean = sem("ln_mean")
        ln_cent = sem("ln_cent")
        ln_sq = sem("ln_sq")
        ln_var = sem("ln_var")
        ln_r = sem("ln_r")
        ln_scaled = sem("ln_scaled")
        z_done = sem("z_done")
        zhi_done = sem("zhi_done")
        z_ready = sem("z_ready")
        act_order = sem("act_order")
        dve_order = sem("dve_order")
        pool_order = sem("pool_order")

        block = ctx.enter_context(nc.Block())

        def x_targets(t):
            if t == 0:
                return [(x_hi, x_lo, G_MIX_PRE)]
            if t == 2:
                return [(x_hi, x_lo, G_KV), (mix_hi, mix_lo, G_MIX_PRE + KC)]
            return [(x_hi, x_lo, {1: G_FFN_PRE, 3: G_FFN_PRE + KC, 4: G2_MIX_PRE, 5: G2_FFN_PRE}[t])]

        def gain(col):
            return par_s[:, col:col + 1]

        @block.sync
        def _(sp):
            for p in range(2):
                sp.dma_start(w_raw[p][:], w_all[p]).then_inc(w_landed[p], 16)
            with sp.Fori(1, UNITS // 2) as i:
                for p in range(2):
                    sp.wait_ge(w_split, 2 * i + (p - 1))
                    sp.dma_start(w_raw[p][:], w_all[2 * i + p]).then_inc(w_landed[p], 16)
            sp.wait_ge(w_split, UNITS - 2)
            sp.dma_start(w_raw[0][:], w_all[UNITS - 1]).then_inc(w_landed[0], 16)
            for m in range(KC):
                sp.wait_ge(h_ready, KC * 5 + m + 1)
                sp.dma_start(out_t[m], h[:, m, :]).then_inc(out_written, 16)
            sp.wait_ge(out_written, 16 * KC)

        @block.gpsimd
        def _(pool):
            pool.memset(ones[:], 1.0).then_inc(consts_ready, 1)
            pool.memset(eps_t[:], EPS).then_inc(consts_ready, 1)
            pool.wait_ge(b_rowcopied, 1)
            pool.dma_start(skew, erow[0:8, :].unsqueeze(1).to_broadcast([8, P, 384])).then_inc(skew_written, 16)
            pool.wait_ge(skew_written, 16)
            pool.wait_ge(xr_ready, 5)
            for n in range(8):
                flat = skew[n].rearrange("q x -> (q x)")[127:127 + P * 383]
                pool.dma_start(bias2[:, n, :], flat.rearrange("(q x) -> q x", x=383)[:, 0:256]).then_inc(bias_loaded, 16)
            pool.dma_start(par2_s[:], par2).then_inc(par2_loaded, 16)

        @block.scalar
        def _(act):
            order = SelfOrder(act, act_order)

            def round_unit(u, i=None, per=0):
                p = u % 2
                act.wait_ge(w_landed[p], run(i, 8 * per, 16 * (u // 2 + 1)))
                if u >= 2:
                    act.wait_ge(unit_done, run(i, per, u - 1))
                nc.scalar.activation(w_hi[p][:], w_raw[p][:], ACT.Copy).then_inc(w_rounded, 1)

            def rstd(stat, out, width, ready):
                order.link(nc.scalar.activation(out, stat, ACT.Ln, bias=eps_t[:], scale=1.0 / width))
                nc.scalar.activation(out, out, ACT.Exp, scale=-0.5).then_inc(ready, 1)

            def post_norm(t):
                for m in range(KC):
                    act.wait_ge(y_copied, KC * (t - 1) + m + 1)
                    if m >= 3:
                        act.wait_ge(yacc_done, 6 * (t - 1) + m - 2)
                    dst = work[:, ACC if m == 0 else 1 + m % 2, :]
                    nc.scalar.activation(dst, y[:, m, :], ACT.Square).then_inc(ysq_done, 1)
                if LAST_ROWS[t] + 2 < UNITS:
                    round_unit(LAST_ROWS[t] + 2)
                nc.scalar.preload_act_table_set("natural_log_exp_and_others")
                act.wait_ge(ystat_done, t)
                rstd(bank[0][:], work[:, RQ, :], D, yr_ready)

            def pre_norm(t):
                for m in range(KC):
                    if t == 0:
                        act.wait_ge(h_loaded, 16)
                    else:
                        act.wait_ge(h_ready, KC * (t - 1) + m + 1)
                    for hi, _, col in x_targets(t):
                        nc.scalar.activation(hi[:, m, :], h[:, m, :], ACT.Copy,
                                             scale=gain(col + m)).then_inc(xhi_done, 1)
                    if m >= 3:
                        act.wait_ge(xacc_done, 7 * t + m - 2)
                    dst = work[:, ACC if m == 0 else 1 + m % 2, :]
                    nc.scalar.activation(dst, h[:, m, :], ACT.Square).then_inc(xsq_done, 1)
                if t != 2:
                    round_unit(LAST_ROWS[t] + 3 if t else 2)
                act.wait_ge(xstat_done, t + 1)
                rstd(bank[3][:], r_pre[:], D, xr_ready)

            def ffn(u0, ev, n, sil):
                def pair(l, i=None, first=False):
                    act.wait_ge(evac, run(i, 4, ev + l + 1))
                    for m in range(2):
                        nc.scalar.activation(work[:, 2 + m, :], work[:, m, :], ACT.Silu).then_inc(silu_done, 1)
                    if not first:
                        round_unit(u0 + l + 2, i, 4)
                    for m in range(2):
                        act.wait_ge(fff_ready, run(i, 4, sil + l + m + 1))
                        c = l + m if i is None else 4 * i + (l + m)
                        nc.scalar.activation(ff_hi[:, c, :], work[:, 4 + m, :], ACT.Copy).then_inc(ffhi_done, 1)
                    round_unit(u0 + l + 3, i, 4)

                nc.scalar.preload_act_table(ACT.Silu)
                pair(0, first=True)
                with act.Fori(0, (FC - 2) // 4) as i:
                    pair(2, i)
                    pair(4, i)

            def down(u0):
                with act.Fori(0, 4) as i:
                    for l in range(2):
                        round_unit(u0 + l + 2, i, 2)
                for l in (8, 9):
                    if u0 + l + 2 < UNITS:
                        round_unit(u0 + l + 2)

            act.dma_start(h[:], x_t.rearrange("m p s -> p m s")).then_inc(h_loaded, 16)
            act.dma_start(par_s[:], par).then_inc(par_loaded, 16)
            act.dma_start(ident[:], ident_c).then_inc(par_loaded, 16)
            act.dma_start(zr[:], zr_c).then_inc(par_loaded, 16)
            act.dma_start(mask_f[:], masks).then_inc(par_loaded, 16)
            act.dma_start(rel_s[0:33, :], rel).then_inc(par_loaded, 16)
            act.dma_start(onehot_s[0:33, :], onehot).then_inc(par_loaded, 16)
            act.dma_start(pos_i[:], pos.to_broadcast([P, S])).then_inc(par_loaded, 16)
            act.wait_ge(par_loaded, 16 * 7)
            act.wait_ge(consts_ready, 2)
            round_unit(0)
            round_unit(1)
            pre_norm(0)
            for n, dst in enumerate((sin_t, cos_t)):
                act.wait_ge(angle_ready, n + 1)
                nc.scalar.activation(dst[:], (work[:, 4, :], work[:, 5, :])[n], ACT.Sin).then_inc(trig_done, 1)

            for l in range(12):
                if l % 3 == 2:
                    for m in range(2):
                        b = 2 * (l // 3) + m
                        act.wait_ge(mixf_ready, b + 1)
                        nc.scalar.activation(mix_hi[:, b, :], cg[:, m, :], ACT.Copy).then_inc(mixhi_done, 1)
                if l:
                    round_unit(l + 2)
            for l in range(3):
                round_unit(CONV_OUT + l + 2)
            post_norm(1)
            pre_norm(1)
            ffn(FFN_A, EV_FFN_A, 0, 0)
            down(DOWN_A)
            post_norm(2)
            pre_norm(2)

            nc.scalar.preload_act_table_set("natural_log_exp_and_others")
            with act.Fori(0, 2) as i:
                for half in range(2):
                    for lam in range(9):
                        round_unit(QKV + 9 * half + lam + 2, i, 18)
                    for pair in range(2):
                        g = 2 * half + pair

                        def cnt(per, v, i=i, g=g):
                            return run(i, 4 * per, per * g + v)

                        act.wait_ge(at_out, cnt(2, 0))
                        for it in range(8):
                            for a in range(2):
                                act.wait_ge(at_scores, cnt(16, 2 * it + a + 1))
                                lo = P if it == 0 else 0
                                src = bank[2 * (it % 2) + a][:, lo:256]
                                if it < 4:
                                    act.wait_ge(at_negmax, cnt(12, 2 * it + a + 1))
                                    nc.scalar.activation(p0[:, a, it, lo:256], src, ACT.Exp,
                                                         bias=nm0[:, 2 * it + a:2 * it + a + 1]).then_inc(at_exp, 1)
                                else:
                                    act.wait_ge(at_negmax, cnt(12, 8 + it - 3))
                                    if it > 4:
                                        act.wait_ge(at_trans, cnt(16, 2 * (it - 5) + a + 1))
                                    n = 2 * (it - 4) + a
                                    nc.scalar.activation(pq[:, a, :], src, ACT.Exp,
                                                         bias=nm[:, n:n + 1]).then_inc(at_exp, 1)
                        act.wait_ge(at_diff, cnt(1, 1))
                        nc.scalar.activation(c0, cdiff, ACT.Exp).then_inc(at_c0, 1)
                        for a in range(2):
                            act.wait_ge(at_av, cnt(16, 15 + a))
                            l_rows = slice(HD, P) if a == 0 else slice(0, HD)
                            o_rows = slice(0, HD) if a == 0 else slice(HD, P)
                            nc.scalar.activation(ln_l[o_rows, a, :], bank[6 + a][l_rows, :], ACT.Ln).then_inc(at_rl, 1)
                            act.wait_ge(at_rl, cnt(4, 2 * a + 1))
                            nc.scalar.activation(ln_l[o_rows, a, :], ln_l[o_rows, a, :], ACT.Exp,
                                                 scale=-1.0).then_inc(at_rl, 1)
            for b in range(KC):
                act.wait_ge(at_out, 16 if b == 7 else 2 * b + 2)
                nc.scalar.activation(mix_hi[:, b, :], o_t[:, b, :], ACT.Copy).then_inc(mixhi_done, 1)
            for l in range(3):
                round_unit(ATT_OUT + l + 2)
            post_norm(3)
            pre_norm(3)
            ffn(FFN_B, EV_FFN_B, 1, FC)
            down(DOWN_B)
            post_norm(4)
            pre_norm(4)

            for l in range(7):
                if l in (1, 3):
                    for m in range(2):
                        act.wait_ge(evac, EV_IN2 + l + 1)
                        nc.scalar.activation(work[:, 4 + m, :], work[:, 2 + m, :], ACT.Sigmoid).then_inc(sig_done, 1)
                if l:
                    round_unit(IN2 + l + 2)
            for t in range(4):
                for hh in range(8):
                    act.wait_ge(b_negmax, t + 1)
                    lo = P if t == 0 else 0
                    if t:
                        act.wait_ge(b_trans, 2 * t)
                    nc.scalar.activation(p2[:, hh, lo:256], t2[:, hh, lo:256], ACT.Exp, bias=nm2[:, hh:hh + 1],
                                         accum_out=l2[:, hh:hh + 1]).then_inc(b_exp, 1)
                nc.scalar.activation(es2, es2, ACT.Exp).then_inc(b_exp, 1)
                act.wait_ge(b_av, t + 1)
                nc.scalar.activation(mix_hi[:, 0:4, t * P:(t + 1) * P],
                                     bank[6 + t % 2][:].rearrange("p (b c) -> p b c", b=4),
                                     ACT.Copy).then_inc(mixhi_done, 1)
            act.wait_ge(ln_sum, 1)
            nc.scalar.activation(work[:, 4, :], bank[0][:], ACT.Copy, scale=1.0 / C2).then_inc(ln_mean, 1)
            for b in range(CB):
                act.wait_ge(ln_cent, b + 1)
                nc.scalar.activation(work[:, b, :], c2[:, b, :], ACT.Square).then_inc(ln_sq, 1)
            act.wait_ge(ln_var, 1)
            rstd(bank[1][:], work[:, 5, :], C2, ln_r)
            for b in range(CB):
                act.wait_ge(ln_scaled, b + 1)
                nc.scalar.activation(c2[:, b, :], c2[:, b, :], ACT.Silu, bias=par2_s[:, LNB + b:LNB + b + 1],
                                     scale=par2_s[:, LNG + b:LNG + b + 1]).then_inc(z_done, 1)
            for b in range(CB):
                act.wait_ge(z_done, b + 1)
                nc.scalar.activation(x_hi[:, b, :], c2[:, b, :], ACT.Copy).then_inc(zhi_done, 1)
            act.wait_ge(unit_done, PW2 + 1)
            for m in range(4):
                nc.scalar.activation(mix_hi[:, 4 + m, :], bank[m][:], ACT.Copy).then_inc(mixhi_done, 1)
            round_unit(PW2 + 2)
            for l in range(3):
                round_unit(OUT2 + l + 2)
            post_norm(5)
            pre_norm(5)
            ffn(FFN_C, EV_FFN_C, 2, 2 * FC)
            down(DOWN_C)
            post_norm(6)

        @block.vector
        def _(dve):
            order = SelfOrder(dve, dve_order)
            v = nc.vector

            def rest_unit(u, i=None, per=0):
                p = u % 2
                dve.wait_ge(w_rounded, run(i, per, u + 1))
                v.tensor_tensor(w_lo[p][:], w_raw[p][:], w_hi[p][:].bitcast(F32), ALU.subtract).then_inc(w_split, 1)

            def xlo(t, m):
                for n, (hi, lo, col) in enumerate(x_targets(t)):
                    dve.wait_ge(xhi_done, X_BASE[t] + X_COUNT[t] * m + n + 1)
                    v.scalar_tensor_tensor(lo[:, m, :], h[:, m, :], gain(col + m), hi[:, m, :].bitcast(F32),
                                           ALU.mult, ALU.subtract).then_inc(x_ready, 1)

            def xadd(t, m):
                if m < 1:
                    return
                dve.wait_ge(xsq_done, KC * t + m + 1)
                if m > 1:
                    dve.wait_ge(xacc_done, 7 * t + m - 1)
                v.tensor_tensor(work[:, ACC, :], work[:, ACC, :], work[:, 1 + m % 2, :], ALU.add).then_inc(xacc_done, 1)

            def post_norm(t):
                last = LAST_ROWS[t]
                for m in range(KC):
                    if m < KC - 1:
                        dve.wait_ge(y_done, 7 * (t - 1) + m + 1)
                    else:
                        dve.wait_ge(unit_done, last + 1)
                    v.tensor_copy(y[:, m, :], bank[m][:]).then_inc(y_copied, 1)
                    if m >= 2:
                        dve.wait_ge(ysq_done, KC * (t - 1) + m)
                        if m > 2:
                            dve.wait_ge(yacc_done, 6 * (t - 1) + m - 2)
                        v.tensor_tensor(work[:, ACC, :], work[:, ACC, :], work[:, 1 + (m - 1) % 2, :],
                                        ALU.add).then_inc(yacc_done, 1)
                if last + 2 < UNITS:
                    rest_unit(last + 2)
                dve.wait_ge(yr_ready, t)

            def residual(t, m):
                order.link(v.scalar_tensor_tensor(work[:, TMP + m % 2, :], y[:, m, :], gain(POST_GAIN[t] + m),
                                                  work[:, RQ, :], ALU.mult, ALU.mult))
                v.tensor_tensor(h[:, m, :], h[:, m, :], work[:, TMP + m % 2, :], ALU.add).then_inc(h_ready, 1)

            def transition(t):
                if t:
                    post_norm(t)
                for m in range(KC):
                    if t:
                        residual(t, m)
                    if t < 6 and m >= 1:
                        xlo(t, m - 1)
                    if t < 6 and m >= 2:
                        xadd(t, m - 2)
                if t < 6:
                    xlo(t, KC - 1)
                    xadd(t, KC - 2)
                    xadd(t, KC - 1)
                    if t != 2:
                        rest_unit(LAST_ROWS[t] + 3 if t else 2)

            def scaled(dst, src, r=None):
                return v.tensor_tensor(dst, src, r_pre[:] if r is None else r, ALU.mult)

            def banks_of(l):
                n = 2 * ((l + 2) % 4)
                return bank[n], bank[n + 1]

            def ffn(u0, ev, t, sil):
                def pair(l, i=None, first=False):
                    dve.wait_ge(unit_done, run(i, 4, u0 + l + 1))
                    b = banks_of(l)
                    scaled(work[:, 0, :], b[0][:])
                    scaled(work[:, 1, :], b[1][:]).then_inc(evac, 1)
                    if not first:
                        rest_unit(u0 + l + 2, i, 4)
                    dve.wait_ge(unit_done, run(i, 4, u0 + l + 2))
                    b = banks_of(l + 1)
                    order.mark(scaled(work[:, 4, :], b[0][:]))
                    scaled(work[:, 5, :], b[1][:]).then_inc(evac, 1)
                    dve.wait_ge(silu_done, run(i, 4, sil + l + 2))
                    order.wait()
                    v.tensor_tensor(work[:, 4, :], work[:, 4, :], work[:, 2, :], ALU.mult).then_inc(fff_ready, 1)
                    dve.wait_ge(evac, run(i, 4, ev + l + 2))
                    v.tensor_tensor(work[:, 5, :], work[:, 5, :], work[:, 3, :], ALU.mult).then_inc(fff_ready, 1)
                    rest_unit(u0 + l + 3, i, 4)
                    for m in range(2):
                        dve.wait_ge(ffhi_done, run(i, 4, sil + l + m + 1))
                        c = l + m if i is None else 4 * i + (l + m)
                        v.tensor_tensor(ff_lo[:, c, :], work[:, 4 + m, :], ff_hi[:, c, :].bitcast(F32),
                                        ALU.subtract).then_inc(ff_ready, 1)

                dve.wait_ge(xr_ready, t + 1)
                pair(0, first=True)
                with dve.Fori(0, (FC - 2) // 4) as i:
                    order.enter(i, 2)
                    pair(2, i)
                    pair(4, i)
                order.leave((FC - 2) // 4)

            def down(u0):
                with dve.Fori(0, 4) as i:
                    for l in range(2):
                        rest_unit(u0 + l + 2, i, 2)
                for l in (8, 9):
                    if u0 + l + 2 < UNITS:
                        rest_unit(u0 + l + 2)

            dve.wait_ge(par_loaded, 16 * 7)
            dve.wait_ge(h_loaded, 16)
            v.tensor_copy(mask_b[:], mask_f[:]).then_inc(casts_ready, 1)
            v.tensor_copy(ident_b[:], ident[:]).then_inc(casts_ready, 1)
            rest_unit(0)
            rest_unit(1)
            transition(0)
            order.link(v.tensor_copy(work[:, 3, :], pos_i[:]))
            order.link(v.tensor_scalar(ang[:], work[:, 3, :], gain(INV_FREQ), None, ALU.mult))
            for n in range(2):
                r = work[:, 4 + n, :]
                order.link(v.tensor_scalar(turn[:], ang[:], 1.0 / (2 * math.pi), 0.25 * n, ALU.mult, ALU.add))
                src = ang[:]
                for part in (TWO_PI_1, TWO_PI_2, TWO_PI_3):
                    order.link(v.scalar_tensor_tensor(r, turn[:], -part, src, ALU.mult, ALU.add))
                    src = r
                order.link(v.tensor_scalar(r, r, 0.5 * math.pi * n, PI_CLAMP, ALU.add, ALU.min))
                v.tensor_scalar(r, r, -PI_CLAMP, None, ALU.max).then_inc(angle_ready, 1)
            dve.wait_ge(b_row, 1)
            v.tensor_copy(erow[0:8, :], bank[2][0:8, 0:384]).then_inc(b_rowcopied, 1)
            dve.wait_ge(trig_done, 2)
            dve.wait_ge(skew_written, 16)

            order.link(v.memset(u1[:, :, 0:2], 0.0))
            dve.wait_ge(xr_ready, 1)
            for l in range(12):
                g3 = l // 3
                dve.wait_ge(unit_done, l + 1)
                b = banks_of(l)
                if l % 3 == 0:
                    if l == 0:
                        order.link(v.tensor_tensor(work[:, 2, :], r_pre[:], r_pre[:], ALU.mult))
                    for m in range(2):
                        ins = scaled(work[:, m, :], b[m][:], work[:, 2, :])
                        if m:
                            ins.then_inc(evac, 1)
                        else:
                            order.mark(ins)
                elif l % 3 == 1:
                    dve.wait_ge(evac, l)
                    for m in range(2):
                        ins = scaled(u1[:, m, 2:S + 2], b[m][:], work[:, m, :])
                        if m:
                            ins.then_inc(evac, 1)
                        else:
                            order.mark(ins)
                    dve.wait_ge(evac, l + 1)
                    order.wait()
                    for tap in range(TAPS1):
                        for m in range(2):
                            w = gain(CONVW + tap * KC + 2 * g3 + m)
                            src = u1[:, m, tap:tap + S]
                            if tap == 0:
                                ins = v.tensor_scalar(cv[:, m, :], src, w, None, ALU.mult)
                            else:
                                order.wait(1)
                                ins = v.scalar_tensor_tensor(cv[:, m, :], src, w, cv[:, m, :], ALU.mult, ALU.add)
                            order.mark(ins)
                else:
                    if g3:
                        dve.wait_ge(mixhi_done, 2 * g3)
                    for m in range(2):
                        ins = scaled(cg[:, m, :], b[m][:])
                        if m:
                            ins.then_inc(evac, 1)
                        else:
                            order.mark(ins)
                    order.wait()
                    dve.wait_ge(evac, l + 1)
                    for m in range(2):
                        v.tensor_tensor(cg[:, m, :], cg[:, m, :], cv[:, m, :], ALU.mult).then_inc(mixf_ready, 1)
                    for m in range(2):
                        c = 2 * g3 + m
                        dve.wait_ge(mixhi_done, c + 1)
                        v.tensor_tensor(mix_lo[:, c, :], cg[:, m, :], mix_hi[:, c, :].bitcast(F32),
                                        ALU.subtract).then_inc(mix_ready, 1)
                if l:
                    rest_unit(l + 2)
            for l in range(3):
                rest_unit(CONV_OUT + l + 2)
            transition(1)
            ffn(FFN_A, EV_FFN_A, 1, 0)
            down(DOWN_A)
            transition(2)

            dve.wait_ge(xr_ready, 3)
            v.tensor_tensor(cos_t[:], cos_t[:], r_pre[:], ALU.mult)
            order.mark(v.tensor_tensor(sin_t[:], sin_t[:], r_pre[:], ALU.mult))
            dve.wait_ge(rcol_ps, 1)
            v.tensor_copy(r_col[:], bank[2][:, 0:8]).then_inc(rcol_ready, 1)
            v.memset(cm, 0.0)
            for b in range(3):
                order.mark(v.memset(v1s[b][:, :, :, HD:2 * HD], 1.0))
            order.wait()
            dve.wait_ge(rcol_ready, 1)
            with dve.Fori(0, 2) as i:
                order.enter(i, 2 * (6 * 3 + 2 * 6))
                for half in range(2):
                    for lam in range(9):
                        u = QKV + 9 * half + lam
                        dve.wait_ge(unit_done, run(i, 18, u + 1))
                        b = banks_of(lam)
                        if lam < 6:
                            br, is_k = lam // 2, lam % 2
                            f = 1.0 if is_k else HD ** -0.5
                            dst = [qk[:, 4 * br + 2 * is_k + n, :] for n in range(2)]
                            if br:
                                dst = [d.rearrange("p (r n) -> p n r", r=4) for d in dst]

                            def part(slot, which, table):
                                return v.scalar_tensor_tensor(work[:, slot, :], b[which][:], f, table[:],
                                                              ALU.mult, ALU.mult)

                            def seen(slot):
                                w_ = work[:, slot, :]
                                return w_.rearrange("p (n r) -> p n r", r=4) if br else w_

                            order.wait()
                            part(0, 0, cos_t)
                            order.mark(part(1, 1, sin_t))
                            part(2, 1, cos_t)
                            part(3, 0, sin_t).then_inc(evac, 1)
                            order.wait()
                            order.mark(v.tensor_tensor(dst[0], seen(0), seen(1), ALU.subtract))
                            dve.wait_ge(evac, run(i, 18, EV_QKV + 9 * half + lam + 1))
                            order.mark(v.tensor_tensor(dst[1], seen(2), seen(3), ALU.add))
                        else:
                            br = lam - 6
                            for t in range(4):
                                src = b[t // 2][:, (t % 2) * 256:(t % 2) * 256 + 256]
                                src = src.rearrange("p (a c d) -> p a c d", a=2, c=2)
                                col = r_col[:, (4 if br == 0 else 0) + t:(4 if br == 0 else 0) + t + 1]
                                dst = v1s[br][:, t, :, :].rearrange("p a (c d) -> p a c d", c=3)[:, :, 0:3:2, :]
                                ins = v.tensor_scalar(dst, src, col, None, ALU.mult)
                            ins.then_inc(evac, 1)
                        rest_unit(u + 2, i, 18)
                    for pair in range(2):
                        g = 2 * half + pair

                        def cnt(per, val, i=i, g=g):
                            return run(i, 4 * per, per * g + val)

                        def pt_copy(it, k):
                            for a in range(2):
                                dve.wait_ge(at_trans, cnt(16, 2 * k + a + 1))
                                if k:
                                    dve.wait_ge(at_av, cnt(16, 2 * (k - 1) + a + 1))
                                lo = P if it == 0 else 0
                                if it < 4:
                                    c = (256 - lo) // P
                                    src = bank[4 + a][:, lo:256].rearrange("p (c i r) -> p c r i", c=c, r=4)
                                    dst = pt[:, a, lo:256].rearrange("p (c r i) -> p c r i", c=c, r=4)
                                    if c == 1:
                                        v.tensor_copy(dst[:, 0], src[:, 0]).then_inc(at_ptcopy, 1)
                                    else:
                                        v.tensor_copy(dst, src).then_inc(at_ptcopy, 1)
                                else:
                                    v.tensor_copy(pt[:, a, :], bank[4 + a][:, 0:256]).then_inc(at_ptcopy, 1)

                        for it in range(4):
                            lo = P if it == 0 else 0
                            for a in range(2):
                                dve.wait_ge(at_scores, cnt(16, 2 * it + a + 1))
                                v.tensor_reduce(nm0[:, 2 * it + a:2 * it + a + 1], bank[2 * (it % 2) + a][:, lo:256],
                                                AX.X, ALU.max, negate=True).then_inc(at_negmax, 1)
                        dve.wait_ge(at_perm, cnt(2, 1))
                        order.link(v.tensor_copy(nm0r, bank[4][:, 0:8]))
                        for it in range(4, 8):
                            n = 2 * (it - 4)
                            for a in range(2):
                                dve.wait_ge(at_scores, cnt(16, 2 * it + a + 1))
                                ins = v.tensor_reduce(nm[:, n + a:n + a + 1], bank[2 * (it % 2) + a][:, 0:256],
                                                      AX.X, ALU.max, negate=True)
                            order.link(ins)
                            v.tensor_tensor(nm[:, n:n + 2], nm[:, n:n + 2], nm0r[:, n:n + 2],
                                            ALU.min).then_inc(at_negmax, 1)
                            if it > 4:
                                pt_copy(it - 1, it - 5)
                        dve.wait_ge(at_negmax, cnt(12, 12))
                        v.tensor_tensor(cdiff, nm, nm0r, ALU.subtract).then_inc(at_diff, 1)
                        pt_copy(7, 3)
                        dve.wait_ge(at_c0, cnt(1, 1))
                        for j in range(4):
                            rows = slice(32 * j, 32 * j + 32)
                            dst = cm[rows, :].rearrange("p (r j a) -> p r j a", r=4, j=4)[:, :, j, :]
                            ins = v.tensor_copy(dst, c0[rows, :].rearrange("p (r a) -> p r a", r=4))
                        ins.then_inc(at_cm, 1)
                        dve.wait_ge(at_perm, cnt(2, 2))
                        order.link(v.tensor_copy(c0n, bank[5][:, 0:8]))
                        for t in range(4):
                            lo = P if t == 0 else 0
                            for a in range(2):
                                dve.wait_ge(at_exp, cnt(16, 2 * t + a + 1))
                                v.tensor_scalar(p0[:, a, t, lo:256], p0[:, a, t, lo:256],
                                                c0n[:, 2 * t + a:2 * t + a + 1], None, ALU.mult).then_inc(at_scaled, 1)
                        for t in range(4):
                            pt_copy(t, 4 + t)
                        for a in range(2):
                            dve.wait_ge(at_rl, cnt(4, 2 * a + 2))
                            rows = slice(0, HD) if a == 0 else slice(HD, P)
                            blk = g if i is None else 4 * i + g
                            dst = o_t[rows, blk, :].rearrange("p (n r) -> p r n", r=4)
                            v.tensor_tensor(dst, bank[6 + a][rows, :].rearrange("p (r n) -> p r n", r=4),
                                            ln_l[rows, a, :].rearrange("p (r n) -> p r n", r=4),
                                            ALU.mult).then_inc(at_out, 1)
            order.leave(2)
            for b in range(KC):
                dve.wait_ge(mixhi_done, KC + b + 1)
                v.tensor_tensor(mix_lo[:, b, :], o_t[:, b, :], mix_hi[:, b, :].bitcast(F32),
                                ALU.subtract).then_inc(mix_ready, 1)
            for l in range(3):
                rest_unit(ATT_OUT + l + 2)
            transition(3)
            ffn(FFN_B, EV_FFN_B, 3, FC)
            down(DOWN_B)
            transition(4)


            order.mark(v.memset(u2[:, :, 0:TAPS2 - 1], 0.0))
            dve.wait_ge(par2_loaded, 16)
            dve.wait_ge(bias_loaded, 16 * 8)
            order.mark(v.tensor_scalar(nsink, par2_s[:, SINK:SINK + 8], -1.0, None, ALU.mult))
            order.wait()
            dve.wait_ge(xr_ready, 5)
            taps = [(tap, b0 + b) for b0 in (0, 2) for tap in range(TAPS2) for b in range(2)]

            def conv_taps(n):
                for _ in range(n):
                    tap, b = taps.pop(0)
                    w = par2_s[:, CDW + tap * CB + b:CDW + tap * CB + b + 1]
                    src = u2[:, b, tap:tap + S]
                    if tap == 0:
                        ins = v.tensor_scalar(c2[:, b, :], src, w, par2_s[:, CDB + b:CDB + b + 1], ALU.mult, ALU.add)
                    else:
                        order.wait(1)
                        ins = v.scalar_tensor_tensor(c2[:, b, :], src, w, c2[:, b, :], ALU.mult, ALU.add)
                    order.mark(ins)

            for l in range(7):
                dve.wait_ge(unit_done, IN2 + l + 1)
                b = banks_of(l)
                if l in (0, 2):
                    order.mark(scaled(work[:, 0, :], b[0][:]))
                    scaled(work[:, 1, :], b[1][:]).then_inc(evac, 1)
                elif l in (1, 3):
                    scaled(work[:, 2, :], b[0][:])
                    scaled(work[:, 3, :], b[1][:]).then_inc(evac, 1)
                    dve.wait_ge(evac, EV_IN2 + l)
                    order.wait()
                    for m in range(2):
                        dve.wait_ge(sig_done, l + m)
                        ins = v.tensor_tensor(u2[:, l - 1 + m, TAPS2 - 1:TAPS2 - 1 + S], work[:, m, :],
                                              work[:, 4 + m, :], ALU.mult)
                        order.mark(ins)
                elif l in (4, 5):
                    order.mark(scaled(q2[:, 2 * (l - 4), :], b[0][:]))
                    scaled(q2[:, 2 * (l - 4) + 1, :], b[1][:]).then_inc(evac, 1)
                else:
                    dve.wait_ge(rcol_ps, 2)
                    v.tensor_copy(r_col[:, 0:4], bank[2][:, 0:4]).then_inc(rcol_ready, 1)
                    order.mark(scaled(k2[:], b[0][:]))
                    dve.wait_ge(rcol_ready, 2)
                    for t in range(4):
                        ins = v.tensor_scalar(v2[:, t, :], b[1][:, t * P:(t + 1) * P], r_col[:, t:t + 1], None, ALU.mult)
                    ins.then_inc(evac, 1)
                if l:
                    rest_unit(IN2 + l + 2)
                    order.wait()
                    conv_taps(10)

            for t in range(4):
                lo = P if t == 0 else 0
                dve.wait_ge(b_scores, t + 1)
                for n in range(4):
                    ins = v.scalar_tensor_tensor(t2[:, 2 * n:2 * n + 2, lo:256],
                                                 bank[n][:].rearrange("p (h k) -> p h k", h=2)[:, :, lo:256],
                                                 HD ** -0.5, bias2[:, 2 * n:2 * n + 2, lo:256], ALU.mult, ALU.add)
                ins.then_inc(b_logits, 1)
                dve.wait_ge(b_logits, t + 1)
                order.link(v.tensor_reduce(nm2, t2[:, :, lo:256], AX.X, ALU.max, negate=True))
                order.link(v.tensor_tensor(nm2, nm2, nsink, ALU.min))
                v.tensor_tensor(es2, par2_s[:, SINK:SINK + 8], nm2, ALU.add).then_inc(b_negmax, 1)
                conv_taps(16)
                dve.wait_ge(b_exp, 9 * t + 9)
                order.link(v.tensor_tensor(l2, l2, es2, ALU.add))
                order.link(v.reciprocal(rl2, l2))
                v.tensor_tensor(p2[:, :, lo:256], p2[:, :, lo:256],
                                rl2.unsqueeze(2).to_broadcast([P, 8, 256 - lo]), ALU.mult).then_inc(b_prob, 1)
                for rd in range(2):
                    dve.wait_ge(b_trans, 2 * t + rd + 1)
                    if t:
                        dve.wait_ge(b_av, t)
                    for n in range(2):
                        dst = pt2[:, 2 * rd + n, :].rearrange("p (h k) -> p h k", h=2)[:, :, lo:256]
                        v.tensor_copy(dst, bank[4 + n][:].rearrange("p (h k) -> p h k", h=2)[:, :, lo:256])\
                            .then_inc(b_ptcopy, 1)
                dve.wait_ge(mixhi_done, 2 * KC + t + 1)
                cols = slice(t * P, (t + 1) * P)
                v.tensor_tensor(mix_lo[:, 0:4, cols], bank[6 + t % 2][:].rearrange("p (b c) -> p b c", b=4),
                                mix_hi[:, 0:4, cols].bitcast(F32), ALU.subtract).then_inc(mix_ready, 1)

            assert not taps
            order.wait()
            v.tensor_copy(st[:, 40:41], st[:, 0:1]).then_inc(conv_ready, 1)
            dve.wait_ge(ln_mean, 1)
            for b in range(CB):
                v.tensor_tensor(c2[:, b, :], c2[:, b, :], work[:, 4, :], ALU.subtract).then_inc(ln_cent, 1)
            dve.wait_ge(ln_r, 1)
            for b in range(CB):
                dve.wait_ge(ln_cent, b + 1)
                dve.wait_ge(ln_sq, b + 1)
                v.tensor_tensor(c2[:, b, :], c2[:, b, :], work[:, 5, :], ALU.mult).then_inc(ln_scaled, 1)
            for b in range(CB):
                dve.wait_ge(zhi_done, b + 1)
                v.tensor_tensor(x_lo[:, b, :], c2[:, b, :], x_hi[:, b, :].bitcast(F32), ALU.subtract).then_inc(z_ready, 1)
            for m in range(4):
                dve.wait_ge(mixhi_done, 2 * KC + 4 + m + 1)
                v.tensor_tensor(mix_lo[:, 4 + m, :], bank[m][:], mix_hi[:, 4 + m, :].bitcast(F32),
                                ALU.subtract).then_inc(mix_ready, 1)
            rest_unit(PW2 + 2)
            for l in range(3):
                rest_unit(OUT2 + l + 2)
            transition(5)
            ffn(FFN_C, EV_FFN_C, 5, 2 * FC)
            down(DOWN_C)
            transition(6)

        @block.tensor
        def _(pe):
            mm = nc.tensor.matmul

            def products(out, w, hi, lo, start, stop, flip=False):
                pairs = ((w[0], hi), (w[0], lo), (w[1], hi))
                for n, (a, b) in enumerate(pairs):
                    ins = mm(out, b if flip else a, a if flip else b,
                             start=start and n == 0, stop=stop and n == 2)
                return ins

            def weights(u, at, n=P):
                return w_hi[u % 2][:, at:at + n], w_lo[u % 2][:, at:at + n]

            def block_of(u, m, b, ks, hi=None, lo=None):
                hi, lo = (x_hi, x_lo) if hi is None else (hi, lo)
                for k in ks:
                    ins = products(b[m][:], weights(u, k * 256 + m * P), hi[:, k, :], lo[:, k, :], k == 0, k == KC - 1)
                return ins

            def banks_of(l):
                n = 2 * ((l + 2) % 4)
                return bank[n], bank[n + 1]

            def unit(u, l, ev, i=None, per=0, hi=None, lo=None):
                pe.wait_ge(w_split, run(i, per, u + 1))
                if l >= 4:
                    pe.wait_ge(evac, run(i, per, ev + l - 3))
                for m in range(2):
                    ins = block_of(u, m, banks_of(l), range(KC), hi, lo)
                ins.then_inc(unit_done, 1)

            def xstat(t):
                pe.wait_ge(xacc_done, 7 * (t + 1))
                mm(bank[3][:], ones[:], work[:, 0, :], start=True, stop=True).then_inc(xstat_done, 1)

            def first_units(t, u):
                early = 5
                pe.wait_ge(w_split, u + 2)
                for k in range(early):
                    pe.wait_ge(x_ready, X_BASE[t] + k + 1)
                    for l in range(2):
                        for m in range(2):
                            block_of(u + l, m, banks_of(l), [k])
                for l in range(2):
                    for k in range(early, KC):
                        if l == 0:
                            pe.wait_ge(x_ready, X_BASE[t] + k + 1)
                        for m in range(2):
                            ins = block_of(u + l, m, banks_of(l), [k])
                    ins.then_inc(unit_done, 1)
                    if l == 0:
                        xstat(t)
                pe.wait_ge(xr_ready, t + 1)

            def ffn(t, u0, ev):
                first_units(t, u0)
                with pe.Fori(0, (FC - 2) // 4) as i:
                    for l in range(2, 6):
                        pe.wait_ge(w_split, run(i, 4, u0 + l + 1))
                        pe.wait_ge(evac, run(i, 4, ev + max(l - 3, 0)))
                        for m in range(2):
                            ins = block_of(u0 + l, m, banks_of(l), range(KC))
                        ins.then_inc(unit_done, 1)

            def rows(u, c, hi, lo, start=False, i=None):
                pe.wait_ge(w_split, run(i, 2, u + 1))
                for kk in range(2):
                    n = 2 * c + kk if i is None else 2 * 2 * i + (2 * c + kk)
                    for m in range(KC):
                        ins = products(bank[m][:], weights(u, kk * D + m * P), hi[:, n, :], lo[:, n, :],
                                       start and kk == 0, False)
                ins.then_inc(unit_done, 1)

            def last_rows(t, u, c, hi, lo):
                pe.wait_ge(w_split, u + 1)
                for m in range(KC):
                    for kk in range(2):
                        n = 2 * c + kk
                        ins = products(bank[m][:], weights(u, kk * D + m * P), hi[:, n, :], lo[:, n, :], False, kk == 1)
                    if m < KC - 1:
                        ins.then_inc(y_done, 1)
                    else:
                        ins.then_inc(unit_done, 1)
                pe.wait_ge(yacc_done, 6 * t)
                mm(bank[0][:], ones[:], work[:, 0, :], start=True, stop=False)
                pe.wait_ge(ysq_done, KC * t)
                mm(bank[0][:], ones[:], work[:, 2, :], start=False, stop=True).then_inc(ystat_done, 1)

            def down(t, u0, ev, base):
                pe.wait_ge(evac, ev)
                for c in range(2):
                    pe.wait_ge(ff_ready, base + 2 * c + 2)
                    rows(u0 + c, c, ff_hi, ff_lo, start=c == 0)
                with pe.Fori(0, 4) as i:
                    for c in (2, 3):
                        pe.wait_ge(ff_ready, run(i, 4, base + 2 * c + 2))
                        rows(u0 + c, c, ff_hi, ff_lo, i=i)
                pe.wait_ge(ff_ready, base + FC)
                last_rows(t, u0 + 10, 10, ff_hi, ff_lo)

            def projection(t, u0, ev, ready):
                pe.wait_ge(evac, ev)
                for c in range(4):
                    pe.wait_ge(mix_ready, ready[c])
                    if c < 3:
                        rows(u0 + c, c, mix_hi, mix_lo, start=c == 0)
                    else:
                        last_rows(t, u0 + c, c, mix_hi, mix_lo)

            pe.wait_ge(par_loaded, 16 * 7)
            pe.wait_ge(consts_ready, 2)
            pe.wait_ge(casts_ready, 2)
            mm(bank[2][0:8, 0:384], rel_s[0:33, :], onehot_s[0:33, :], start=True, stop=True).then_inc(b_row, 1)

            first_units(0, CONV_IN)
            pe.wait_ge(b_rowcopied, 1)
            for l in range(2, 12):
                unit(CONV_IN + l, l, EV_CONV)
            projection(1, CONV_OUT, EV_FFN_A, [2, 4, 6, 8])
            ffn(1, FFN_A, EV_FFN_A)
            down(2, DOWN_A, EV_QKV, 0)

            xstat(2)
            pe.wait_ge(xr_ready, 3)
            for n in range(8):
                cols = slice(n, S, 4) if n < 4 else slice((n - 4) * P, (n - 3) * P)
                ins = mm(bank[2][:, n:n + 1], r_pre[0:1, cols], ones[0:1, 0:1], start=True, stop=True)
            ins.then_inc(rcol_ps, 1)
            pe.wait_ge(x_ready, X_BASE[3])
            pe.wait_ge(rcol_ready, 1)
            with pe.Fori(0, 2) as i:
                for half in range(2):
                    pe.wait_ge(at_out, run(i, 8, 4 * half))
                    for lam in range(9):
                        u = QKV + 9 * half + lam
                        if lam < 6:
                            q_side = lam % 2 == 0
                            pe.wait_ge(w_split, run(i, 18, u + 1))
                            if lam >= 4:
                                pe.wait_ge(evac, run(i, 18, EV_QKV + 9 * half + lam - 3))
                            for m in range(2):
                                ins = block_of(u, m, banks_of(lam), range(KC), mix_hi if q_side else x_hi,
                                               mix_lo if q_side else x_lo)
                            ins.then_inc(unit_done, 1)
                        else:
                            pe.wait_ge(w_split, run(i, 18, u + 1))
                            pe.wait_ge(evac, run(i, 18, EV_QKV + 9 * half + lam - 3))
                            b = banks_of(lam)
                            for t in range(4):
                                cols = slice(t * P, (t + 1) * P) if lam == 6 else slice(t, S, 4)
                                for k in range(KC):
                                    ins = products(b[t // 2][:, (t % 2) * 256:(t % 2) * 256 + 256],
                                                   weights(u, k * 256, 256), x_hi[:, k, cols], x_lo[:, k, cols],
                                                   k == 0, k == KC - 1, flip=True)
                            ins.then_inc(unit_done, 1)
                    pe.wait_ge(evac, run(i, 18, EV_QKV + 9 * half + 9))
                    pe.wait_ge(w_split, run(i, 18, QKV + 9 * half + 11))
                    for pair in range(2):
                        g = 2 * half + pair

                        def cnt(per, val, i=i, g=g):
                            return run(i, 4 * per, per * g + val)

                        def scores(it):
                            t = it % 4
                            lo = P if it == 0 else 0
                            out = [bank[2 * (it % 2) + a] for a in range(2)]
                            for a in range(2):
                                if it >= 2:
                                    pe.wait_ge(at_exp, cnt(16, 2 * (it - 2) + a + 1))
                                m0 = lo if it < 4 else P
                                mm(out[a][:, lo:256], ident_b[:], mask_b[:, m0:m0 + 256 - lo], start=True, stop=False)
                            parts = [(0, slice((t - 1) * P if t else 0, (t + 1) * P), slice(lo, 256))] if it < 4 else \
                                [(br, slice(t * P, (t + 1) * P), slice((br - 1) * P, br * P)) for br in (1, 2)]
                            for n, (br, keys, cols) in enumerate(parts):
                                for part in range(2):
                                    for a in range(2):
                                        j = 2 * pair + a
                                        rows_ = slice(32 * j, 32 * j + 32)
                                        last = n == len(parts) - 1 and part == 1
                                        ins = mm(out[a][:, cols], qk[rows_, 4 * br + part, t * P:(t + 1) * P],
                                                 qk[rows_, 4 * br + 2 + part, keys], start=False, stop=last)
                                        if last:
                                            ins.then_inc(at_scores, 1)

                        def transposes(it, k):
                            for a in range(2):
                                if it < 4:
                                    pe.wait_ge(at_scaled, cnt(8, 2 * it + a + 1))
                                    src = p0[:, a, it, :]
                                else:
                                    pe.wait_ge(at_exp, cnt(16, 2 * it + a + 1))
                                    src = pq[:, a, :]
                                if k:
                                    pe.wait_ge(at_ptcopy, cnt(16, 2 * (k - 1) + a + 1))
                                for c in range(1 if it == 0 else 0, 2):
                                    ins = nc.tensor.transpose(bank[4 + a][:, c * P:(c + 1) * P],
                                                              src[:, c * P:(c + 1) * P], ident[:])
                                ins.then_inc(at_trans, 1)

                        def values(it, k):
                            for a in range(2):
                                pe.wait_ge(at_ptcopy, cnt(16, 2 * k + a + 1))
                                t = it % 4
                                for c in range(1 if it == 0 else 0, 2):
                                    br = 0 if it < 4 else 1 + c
                                    tile = t - 1 + c if it < 4 else t
                                    vv = v1s[br][:, tile, pair, a * HD:a * HD + P]
                                    rhs = pt[:, a, c * P:(c + 1) * P]
                                    if it < 4:
                                        out = bank[6 + a][:].rearrange("p (r n) -> p r n", r=4)[:, :, 32 * t:32 * t + 32]
                                        rhs = rhs.rearrange("p (r i) -> p r i", r=4)
                                    else:
                                        out = bank[6 + a][:, t * P:(t + 1) * P]
                                    ins = mm(out, vv, rhs, start=k == 0 and c == 0, stop=k == 7 and c == 1,
                                             skip_group_check=True)
                                ins.then_inc(at_av, 1)

                        for it in range(4):
                            scores(it)
                        pe.wait_ge(at_negmax, cnt(12, 8))
                        for r in range(4):
                            for j in range(4):
                                ins = mm(bank[4][32 * j:32 * j + 32, 2 * r:2 * r + 2], ident[:, r::4],
                                         nm0[:, 2 * j:2 * j + 2], start=True, stop=True)
                        ins.then_inc(at_perm, 1)
                        scores(4)
                        scores(5)
                        pe.wait_ge(at_out, cnt(2, 0))
                        for it in range(4, 8):
                            transposes(it, it - 4)
                            if it < 6:
                                scores(it + 2)
                            values(it, it - 4)
                        pe.wait_ge(at_cm, cnt(1, 1))
                        for r in range(4):
                            ins = mm(bank[5][:, 0:8], zr[:, 3 - r:3 - r + P], cm[:, 8 * r:8 * r + 8],
                                     start=r == 0, stop=r == 3)
                        ins.then_inc(at_perm, 1)
                        for t in range(4):
                            transposes(t, 4 + t)
                            values(t, 4 + t)
            projection(3, ATT_OUT, EV_FFN_B, [10, 12, 14, 16])
            ffn(3, FFN_B, EV_FFN_B)
            down(4, DOWN_B, EV_IN2, FC)

            first_units(4, IN2)
            for l in range(2, 6):
                unit(IN2 + l, l, EV_IN2)
            pe.wait_ge(evac, EV_IN2 + 4)
            for t in range(4):
                ins = mm(bank[2][:, t:t + 1], r_pre[0:1, t * P:(t + 1) * P], ones[0:1, 0:1], start=True, stop=True)
            ins.then_inc(rcol_ps, 1)
            u = IN2 + 6
            pe.wait_ge(w_split, u + 1)
            block_of(u, 0, banks_of(6), range(KC))
            for t in range(4):
                for k in range(KC):
                    ins = products(banks_of(6)[1][:, t * P:(t + 1) * P], weights(u, k * 256 + P),
                                   x_hi[:, k, t * P:(t + 1) * P], x_lo[:, k, t * P:(t + 1) * P],
                                   k == 0, k == KC - 1, flip=True)
            ins.then_inc(unit_done, 1)
            pe.wait_ge(evac, EV_IN2 + 7)

            def scores2(t):
                lo = P if t == 0 else 0
                if t:
                    pe.wait_ge(b_logits, t)
                for b in range(4):
                    for kv in range(2):
                        rows_ = slice(HD * kv, HD * kv + HD)
                        at = (b % 2) * 256
                        ins = mm(bank[2 * kv + b // 2][:, at + lo:at + 256], q2[rows_, b, t * P:(t + 1) * P],
                                 k2[rows_, (t - 1) * P + lo:(t + 1) * P], start=True, stop=True)
                ins.then_inc(b_scores, 1)

            scores2(0)
            for t in range(4):
                if t < 3:
                    scores2(t + 1)
                pe.wait_ge(b_prob, t + 1)
                for rd in range(2):
                    if t or rd:
                        pe.wait_ge(b_ptcopy, 4 * t + 2 * rd)
                    for hh in range(4):
                        for c in range(1 if t == 0 else 0, 2):
                            ins = nc.tensor.transpose(bank[4 + hh // 2][:, (hh % 2) * 256 + c * P:(hh % 2) * 256 + c * P + P],
                                                      p2[:, 4 * rd + hh, c * P:(c + 1) * P], ident[:])
                    ins.then_inc(b_trans, 1)
                if t >= 2:
                    pe.wait_ge(mix_ready, 2 * KC + t - 1)
                for hh in range(8):
                    if hh % 4 == 0:
                        pe.wait_ge(b_ptcopy, 4 * t + 2 * (hh // 4) + 2)
                    kv = hh // 4
                    for c in range(1 if t == 0 else 0, 2):
                        out = bank[6 + t % 2][HD * (hh % 2):HD * (hh % 2) + HD, (hh // 2) * P:(hh // 2 + 1) * P]
                        at = (hh % 2) * 256 + c * P
                        ins = mm(out, v2[:, t - 1 + c, kv * HD:(kv + 1) * HD], pt2[:, hh // 2, at:at + P],
                                 start=c == (1 if t == 0 else 0), stop=c == 1)
                ins.then_inc(b_av, 1)
            pe.wait_ge(conv_ready, 1)
            for b in range(CB):
                ins = mm(bank[0][:], ones[:], c2[:, b, :], start=b == 0, stop=b == CB - 1)
            ins.then_inc(ln_sum, 1)
            for b in range(CB):
                pe.wait_ge(ln_sq, b + 1)
                ins = mm(bank[1][:], ones[:], work[:, b, :], start=b == 0, stop=b == CB - 1)
            ins.then_inc(ln_var, 1)
            pe.wait_ge(w_split, PW2 + 1)
            pe.wait_ge(z_ready, CB)
            for m in range(4):
                for k in range(CB):
                    ins = products(bank[m][:], weights(PW2, k * C2 + m * P), x_hi[:, k, :], x_lo[:, k, :],
                                   k == 0, k == CB - 1)
            ins.then_inc(unit_done, 1)
            projection(5, OUT2, EV_FFN_C, [24, 24, 24, 24])
            ffn(5, FFN_C, EV_FFN_C)
            down(6, DOWN_C, EV_FFN_C + FC, 2 * FC)


def columns_unit(w, cols):
    k = w.shape[0] // P
    return w[:, cols].reshape(k, P, len(cols)).transpose(1, 0, 2).reshape(P, -1)


def rows_units(w):
    k = w.shape[0] // (2 * P)
    return list(w.reshape(k, 2, P, w.shape[1]).transpose(0, 2, 1, 3).reshape(k, P, UNIT))


def weight_units(a):
    r256 = np.arange(256)
    units = []
    w = a["conv_w_in"][0]
    for g in range(4):
        for base in (D, 2 * D, 0):
            units.append(columns_unit(w, base + 256 * g + r256))
    units += rows_units(a["conv_w_out"][0])

    def ffn(gate, up, down):
        for g in range(FC // 2):
            units.append(columns_unit(gate, 256 * g + r256))
            units.append(columns_unit(up, 256 * g + r256))
        units.extend(rows_units(down))

    gu = a["ffn_w_gate_up"]
    ffn(gu[0][:, :D_FF], gu[0][:, D_FF:], a["ffn_w_down"][0])
    halves = np.concatenate([np.arange(32) + HD * j + HALF * n for n in range(2) for j in range(4)])
    q_width = 3 * D
    for hg in range(4):
        for br in range(3):
            base = br * D + 256 * hg
            units.append(columns_unit(a["w_q"][0], base + halves))
            units.append(columns_unit(a["w_kv"], base + halves))
        for br in range(3):
            units.append(columns_unit(a["w_kv"], q_width + br * D + 256 * hg + r256))
    units += rows_units(a["w_o"][0])
    ffn(gu[1][:, :D_FF], gu[1][:, D_FF:], a["ffn_w_down"][1])
    w = a["w_in_2"]
    for g in range(2):
        units.append(columns_unit(w, 768 + 256 * g + r256))
        units.append(columns_unit(w, 768 + C2 + 256 * g + r256))
    r64 = np.arange(HD)
    for g in range(2):
        heads = (2 * g, 2 * g + 4, 2 * g + 1, 2 * g + 5)
        units.append(columns_unit(w, np.concatenate([HD * x + r64 for x in heads])))
    units.append(columns_unit(w, 512 + r256))
    units.append(columns_unit(a["w_conv_pw_2"], np.arange(C2)))
    units += rows_units(a["w_out_2"])
    ffn(a["w_gate_2"], a["w_up_2"], a["w_down_2"])
    assert len(units) == UNITS
    return np.stack(units)


def constants():
    q, k = np.arange(P)[:, None], np.arange(P)[None, :]
    no = np.float32(NEG)
    prev = np.where(k >= q, 0, no)
    causal = np.where(k <= q, 0, no)
    residue = np.where((k <= q) & (k % 4 == q % 4), 0, no)
    masks = np.concatenate([prev, causal, residue], 1).astype(np.float32)
    ident = np.eye(P, dtype=np.float32)
    zr = (np.arange(P + 3)[None, :] == 4 * (q % 32) + 3).astype(np.float32)
    onehot = np.zeros((33, 384), np.float32)
    for x in range(384):
        dist = 255 - x
        if 0 <= dist < 128:
            bucket = dist if dist < 16 else min(31, 16 + int(math.log(dist / 16) / math.log(8) * 16))
            onehot[bucket, x] = 1
        else:
            onehot[32, x] = no
    inv_freq = (np.float32(10000.0) ** (-np.arange(HALF, dtype=np.float32) / HALF)).astype(np.float32)
    return masks, ident, zr, onehot, np.tile(inv_freq, 4)[:, None]


def kernel(**inputs):
    import concourse.bacc as bacc
    from concourse.bass_utils import run_bass_kernel_spmd

    a = {n: np.asarray(x) for n, x in inputs.items()}
    masks, ident, zr, onehot, inv_freq = constants()

    def cols(x):
        return np.asarray(x).reshape(-1, P).T

    par = np.concatenate(
        [cols(a[n]) for n in ("mix_norm_pre", "mix_norm_post", "ffn_norm_pre", "ffn_norm_post", "kv_norm",
                              "mix_pre_g_2", "mix_post_g_2", "ffn_pre_g_2", "ffn_post_g_2")]
        + [cols(a["conv_w"][0]), inv_freq], 1)
    par2 = np.concatenate([cols(a["conv_dw_2"]), cols(a["conv_dw_b_2"]), cols(a["conv_ln_g_2"]),
                           cols(a["conv_ln_b_2"]), np.tile(a["attn_sinks_2"][None, :], (P, 1))], 1)
    arrays = {
        "x_t": np.ascontiguousarray(a["x"][0].T.reshape(KC, P, S)),
        "pos": a["positions"],
        "w_all": weight_units(a),
        "par": np.ascontiguousarray(par),
        "par2": np.ascontiguousarray(par2),
        "masks": masks,
        "ident_c": ident,
        "zr_c": zr,
        "rel": np.concatenate([a["rel_bias_2"], np.ones((1, 8), np.float32)]),
        "onehot": onehot,
    }
    nc = bacc.Bacc("TRN2", target_bir_lowering=False, num_devices=1)
    aps = {n: nc.dram_tensor(n, x.shape, mybir.dt.from_np(x.dtype), kind="ExternalInput").ap()
           for n, x in arrays.items()}
    skew = nc.dram_tensor("skew", (8, P, 384), F32, kind="Internal").ap()
    out_t = nc.dram_tensor("out_t", (KC, P, S), F32, kind="ExternalOutput").ap()
    program(nc, skew=skew, out_t=out_t, **aps)
    r = run_bass_kernel_spmd(nc, [arrays], core_ids=[0])
    return np.ascontiguousarray(np.asarray(r.results[0]["out_t"]).reshape(D, S).T)[None]
```

```python
import math
from contextlib import ExitStack

import numpy as np

import concourse.bass as bass
from concourse import mybir

F32 = mybir.dt.float32
F32R = mybir.dt.float32r
BF16 = mybir.dt.bfloat16
I32 = mybir.dt.int32
ACT = mybir.ActivationFunctionType
ALU = mybir.AluOpType
AX = mybir.AxisListType

P = 128
S = 512
D = 1024
KC = D // P
D_FF = 2816
FC = D_FF // P
HD = 64
HALF = HD // 2
EPS = 1e-6
NEG = -1e30
TAPS1 = 3
TAPS2 = 31
C2 = 512
CB = C2 // P
UNIT = 2048

GROUP = 10
WARM = 30
MOVE = 8 * 16
CONV_IN = 0
CONV_OUT = CONV_IN + 12
FFN_A = CONV_OUT + 4
DOWN_A = FFN_A + FC
QKV = DOWN_A + FC // 2
ATT_OUT = QKV + 4 * GROUP
FFN_B = ATT_OUT + 4
DOWN_B = FFN_B + FC
IN2 = DOWN_B + FC // 2
PW2 = IN2 + 7
OUT2 = PW2 + 1
FFN_C = OUT2 + 4
DOWN_C = FFN_C + FC
UNITS = DOWN_C + FC // 2

EV_CONV, EV_FFN_A = 0, 12
EV_QKV = EV_FFN_A + FC
EV_FFN_B = EV_QKV + 36
EV_IN2 = EV_FFN_B + FC
EV_FFN_C = EV_IN2 + 7

G_MIX_PRE, G_MIX_POST, G_FFN_PRE, G_FFN_POST = 0, 16, 32, 48
G_KV = 64
G2_MIX_PRE, G2_MIX_POST, G2_FFN_PRE, G2_FFN_POST = 72, 80, 88, 96
CONVW = 104
INV_FREQ = CONVW + TAPS1 * KC
PCOLS = INV_FREQ + 1
CDW = 0
CDB = CDW + TAPS2 * CB
LNG = CDB + CB
LNB = LNG + CB
SINK = LNB + CB
P2COLS = SINK + 8

POST_GAIN = [None, G_MIX_POST, G_FFN_POST, G_MIX_POST + KC, G_FFN_POST + KC, G2_MIX_POST, G2_FFN_POST]
LAST_ROWS = [None, FFN_A - 1, QKV - 1, FFN_B - 1, IN2 - 1, FFN_C - 1, UNITS - 1]

PI_CLAMP = 3.1415925
TWO_PI_1, TWO_PI_2, TWO_PI_3 = 6.28125, 1.9350051879882812e-3, 3.0199159819567528e-7


class SelfOrder:

    def __init__(self, eng, sem):
        self.eng, self.sem, self.n, self.i, self.per = eng, sem, 0, None, 0

    def mark(self, ins):
        ins.then_inc(self.sem, 1)
        self.n += 1

    def value(self, back=0):
        v = self.n - back
        return v if self.i is None else self.per * self.i + v

    def wait(self, back=0):
        self.eng.wait_ge(self.sem, self.value(back))

    def link(self, ins):
        self.mark(ins)
        self.wait()

    def enter(self, i, per):
        self.i, self.per, self.start = i, per, self.n

    def leave(self, turns):
        assert self.n - self.start == self.per, (self.n - self.start, self.per)
        self.i = None
        self.n = self.start + self.per * turns


def run(i, per, v):
    return v if i is None else per * i + v


PAIR_STEPS = (["S0"], ["S1"], ["S2"], ["S3"], ["MAXPERM", "S4"], ["T4", "S5"], ["V4", "T5", "S6"],
              ["V5", "T6", "S7"], ["V6", "T7", "FACTOR"], ["V7", "FACTORPERM"], ["T0"], ["V0", "T1"],
              ["V1", "T2"], ["V2", "T3"], ["V3"], ["OUT"])
ITEM_ORDER = {4: 0, 5: 1, 6: 2, 7: 3, 0: 4, 1: 5, 2: 6, 3: 7}
GROUP_STEPS = [(pair, names) for pair in range(2) for names in PAIR_STEPS]


def interleaved(units, chunks):
    done = 0
    for n, (pair, names) in enumerate(GROUP_STEPS):
        for name in names:
            yield "step", pair, name
        upto = units * chunks * (n + 1) // len(GROUP_STEPS)
        while done < upto:
            yield "chunk", done // chunks, done % chunks
            done += 1
            if done % chunks == chunks // 2:
                yield "half_end", done // chunks, None
            if done % chunks == 0:
                yield "unit_end", done // chunks - 1, None


def program(nc, x_t, pos, w_all, par, par2, masks, ident_c, zr_c, rel, onehot, skew, out_t):
    ctx = ExitStack()
    with ctx:
        cursor = [-(-nc.sbuf_base // 32) * 32]

        def sb(name, shape, dt=F32, at=None):
            size = int(np.prod(shape[1:])) * (2 if dt == BF16 else 4)
            if at is None:
                at = cursor[0]
                cursor[0] += -(-size // 32) * 32
            assert at + size <= nc.sbuf_usable_end, (name, at + size)
            return nc.alloc_sbuf_tensor_at(name, shape, dt, offset=at)

        def sem(name):
            return ctx.enter_context(nc.semaphore(name))

        h = sb("h", [P, KC, S])
        w_raw = [sb(f"w_raw{p}", [P, UNIT]) for p in range(2)]
        w_hi = [sb(f"w_hi{p}", [P, UNIT], F32R) for p in range(2)]
        w_lo = [sb(f"w_lo{p}", [P, UNIT], F32R) for p in range(2)]
        x_hi = sb("x_hi", [P, KC, S], F32R)
        x_lo = sb("x_lo", [P, KC, S], F32R)
        region = cursor[0]
        ff_hi = sb("ff_hi", [P, FC, S], F32R)
        ff_lo = sb("ff_lo", [P, FC, S], F32R)
        cursor[0] += 2048
        K16 = KC * S * 4
        y = sb("y", [P, KC, S], at=region)
        mix_hi = sb("mix_hi", [P, KC, S], F32R, at=region + K16)
        mix_lo = sb("mix_lo", [P, KC, S], F32R, at=region + 2 * K16)
        tail = region + 3 * K16
        u1 = sb("u1", [P, 2, S + 2], at=tail)
        cg = sb("cg", [P, 2, S], at=tail + 4160)
        cv = sb("cv", [P, 2, S], at=tail + 4160 + 4096)
        o_t = sb("o_t", [P, KC, S], at=region)
        qk = sb("qk", [P, 12, S], at=tail)
        qk_next = sb("qk_next", [P, 12, S], at=region + K16)
        turned = sb("turned", [P, 4, S], at=region + K16 + 12 * S * 4)
        v_at = tail + 12 * S * 4
        v1s = [sb(f"v1s{b}", [P, 4, 2, 3 * HD], at=v_at + b * 4 * 2 * 3 * HD * 4) for b in range(3)]
        p2s = [sb(f"p2s{n}", [P, 8, 256], at=region + 8192 * n) for n in range(2)]
        q2 = sb("q2", [P, 4, S], at=tail)
        k2 = sb("k2", [P, S], at=tail + 8192)
        v2 = sb("v2", [P, 4, P], at=tail + 8192 + 2048)
        u2_at = tail + 8192 + 4096
        u2 = sb("u2", [P, CB, S + 32], at=u2_at)
        c2_at = u2_at + CB * (S + 32) * 4
        c2 = sb("c2", [P, CB, S], at=c2_at)
        bias2 = sb("bias2", [P, 8, 256], at=c2_at + CB * S * 4)
        par2_s = sb("par2_s", [P, P2COLS], at=c2_at + CB * S * 4 + 8192)
        work_at = cursor[0]
        work = sb("work", [P, 6, S])
        r_pre = sb("r_pre", [P, S])
        cos_t = sb("cos_t", [P, S])
        sin_t = sb("sin_t", [P, S])
        par_s = sb("par_s", [P, PCOLS])
        mask_b = sb("mask_b", [P, 3 * P], BF16)
        ident = sb("ident", [P, P])
        ident_b = sb("ident_b", [P, P], BF16)
        zr = sb("zr", [P, P + 3])
        ones = sb("ones", [P, P])
        eps_t = sb("eps_t", [P, 1])
        r_col = sb("r_col", [P, 8])
        st = sb("st", [P, 96])
        ACC, TMP, RQ = 0, 3, 5
        p0 = sb("p0", [P, 2, 4, 256], at=work_at)
        pq = sb("pq", [P, 2, 256], at=4 * S * 4 + work_at)
        pt = sb("pt", [P, 2, 256], at=5 * S * 4 + work_at)
        ln_l = sb("ln_l", [P, 2, S], at=work_at)
        pt2 = sb("pt2", [P, 4, S], at=work_at)
        nm0, nm0r, nm, c0, c0n, cm, cdiff = (st[:, 0:8], st[:, 8:16], st[:, 16:24], st[:, 24:32],
                                      st[:, 32:40], st[:, 40:72], st[:, 72:80])
        nm2s, l2s, es2s = [[st[:, at + 8 * n:at + 8 * n + 8] for n in range(2)] for at in (0, 16, 32)]
        nsink, rl2 = st[:, 48:56], st[:, 56:64]
        ln_squares = p2s[0]
        tap_out = [cos_t, sin_t]
        rel_s = sb("rel_s", [P, 8], at=region)
        onehot_s = sb("onehot_s", [P, 384], at=region + 64)
        erow = sb("erow", [P, 384], at=region + 2048)
        pos_i = sb("pos_i", [P, S], I32, at=region + 4096)
        ang = sb("ang", [P, S], at=region + 6144)
        turn = sb("turn", [P, S], I32, at=region + 8192)
        mask_f = sb("mask_f", [P, 3 * P], at=region + 10240)

        bank = [ctx.enter_context(nc.psum_tensor(f"bank{i}", [P, S], F32)) for i in range(8)]

        w_landed = [sem(f"w_landed{p}") for p in range(2)]
        w_rounded = sem("w_rounded")
        w_split = sem("w_split")
        unit_done = sem("unit_done")
        evac = sem("evac")
        h_loaded = [sem(f"h_loaded{n}") for n in range(2)]
        par_loaded = sem("par_loaded")
        tables_loaded = sem("tables_loaded")
        par2_loaded = sem("par2_loaded")
        skew_written = sem("skew_written")
        bias_loaded = sem("bias_loaded")
        out_written = sem("out_written")
        consts_ready = sem("consts_ready")
        casts_ready = sem("casts_ready")
        y_done = sem("y_done")
        y_copied = sem("y_copied")
        ysq_done = sem("ysq_done")
        yacc_done = sem("yacc_done")
        ystat_done = sem("ystat_done")
        yr_ready = sem("yr_ready")
        h_ready = sem("h_ready")
        xhi_done = sem("xhi_done")
        x_ready = sem("x_ready")
        xsq_done = sem("xsq_done")
        xacc_done = sem("xacc_done")
        xstat_done = sem("xstat_done")
        xr_ready = sem("xr_ready")
        mixf_ready = sem("mixf_ready")
        mixhi_done = sem("mixhi_done")
        mix_ready = sem("mix_ready")
        silu_done = sem("silu_done")
        fff_ready = sem("fff_ready")
        ffhi_done = sem("ffhi_done")
        ff_ready = sem("ff_ready")
        angle_ready = sem("angle_ready")
        trig_done = sem("trig_done")
        rcol_ps = sem("rcol_ps")
        rcol_ready = sem("rcol_ready")
        half_done = sem("half_done")
        half_read = sem("half_read")
        rope_done = sem("rope_done")
        qk_moved = sem("qk_moved")
        at_scores = sem("at_scores")
        at_negmax = sem("at_negmax")
        at_exp = sem("at_exp")
        at_perm = sem("at_perm")
        at_diff = sem("at_diff")
        at_c0 = sem("at_c0")
        at_cm = sem("at_cm")
        at_scaled = sem("at_scaled")
        at_trans = sem("at_trans")
        at_ptcopy = sem("at_ptcopy")
        at_av = sem("at_av")
        at_rl = sem("at_rl")
        at_out = sem("at_out")
        b_row = sem("b_row")
        b_rowcopied = sem("b_rowcopied")
        b_scores = sem("b_scores")
        b_logits = sem("b_logits")
        b_negmax = sem("b_negmax")
        b_exp = sem("b_exp")
        b_prob = sem("b_prob")
        b_trans = sem("b_trans")
        b_ptcopy = sem("b_ptcopy")
        b_av = sem("b_av")
        sig_done = sem("sig_done")
        conv_ready = sem("conv_ready")
        gated = sem("gated")
        tap_made = sem("tap_made")
        tap_added = sem("tap_added")
        rl2_ready = sem("rl2_ready")
        ln_sum = sem("ln_sum")
        ln_mean = sem("ln_mean")
        ln_cent = sem("ln_cent")
        ln_sq = sem("ln_sq")
        ln_var = sem("ln_var")
        ln_r = sem("ln_r")
        ln_scaled = sem("ln_scaled")
        z_done = sem("z_done")
        zhi_done = sem("zhi_done")
        pw_done = sem("pw_done")
        z_ready = sem("z_ready")
        act_order = sem("act_order")
        dve_order = sem("dve_order")

        block = ctx.enter_context(nc.Block())

        PRE_GAIN = [G_MIX_PRE, G_FFN_PRE, None, G_FFN_PRE + KC, G2_MIX_PRE, G2_FFN_PRE]

        def parts_of(u):
            if not QKV <= u < ATT_OUT:
                return [(slice(0, UNIT), None)]
            lam = (u - QKV) % GROUP
            col = G_MIX_PRE + KC if lam < 6 and lam % 2 == 0 else G_KV
            first, chunks = {8: (0, KC // 2), 9: (KC // 2, KC // 2)}.get(lam, (0, KC))
            return [(slice(256 * k, 256 * k + 256), gain(col + first + k)) for k in range(chunks)]

        def gain(col):
            return par_s[:, col:col + 1]

        def pair_count(i, pair, per, n):
            return per * (6 + pair) + n if i is None else run(i, 2 * per, per * pair + n)

        def v_banks(lam):
            return [(bank[2], bank[3]), (bank[0], bank[1]), (bank[4], bank[5])][lam - 6]

        def score_bank(i, it, a):
            return bank[a if i is not None else 2 * (it % 2) + a]

        @block.sync
        def _(sp):
            for p in range(2):
                sp.dma_start(w_raw[p][:], w_all[p]).then_inc(w_landed[p], 16)
            with sp.Fori(1, UNITS // 2) as i:
                for p in range(2):
                    sp.wait_ge(w_split, 2 * i + (p - 1))
                    sp.dma_start(w_raw[p][:], w_all[2 * i + p]).then_inc(w_landed[p], 16)
            sp.wait_ge(w_split, UNITS - 2)
            sp.dma_start(w_raw[0][:], w_all[UNITS - 1]).then_inc(w_landed[0], 16)
            for m in range(KC):
                sp.wait_ge(h_ready, KC * 5 + m + 1)
                sp.dma_start(out_t[m], h[:, m, :]).then_inc(out_written, 16)
            sp.wait_ge(out_written, 16 * KC)

        @block.gpsimd
        def _(pool):
            pool.memset(ones[:], 1.0).then_inc(consts_ready, 1)
            pool.memset(eps_t[:], EPS).then_inc(consts_ready, 1)
            pool.wait_ge(b_rowcopied, 1)
            pool.dma_start(skew, erow[0:8, :].unsqueeze(1).to_broadcast([8, P, 384])).then_inc(skew_written, 16)
            pool.wait_ge(skew_written, 16)
            pool.wait_ge(unit_done, IN2)
            pool.dma_start(par2_s[:], par2).then_inc(par2_loaded, 16)
            for n in range(8):
                flat = skew[n].rearrange("q x -> (q x)")[127:127 + P * 383]
                pool.dma_start(bias2[:, n, :], flat.rearrange("(q x) -> q x", x=383)[:, 0:256]).then_inc(bias_loaded, 16)
            for b in range(2):
                for tap in range(1, TAPS2):
                    pool.wait_ge(tap_made, TAPS2 * b + tap + 1)
                    if tap > 1:
                        pool.wait_ge(tap_added, (TAPS2 - 1) * b + tap - 1)
                    nc.gpsimd.tensor_tensor(c2[:, b, :], c2[:, b, :], tap_out[tap % 2][:],
                                            ALU.add).then_inc(tap_added, 1)

        @block.scalar
        def _(act):
            order = SelfOrder(act, act_order)

            def round_unit(u, i=None, per=0):
                p = u % 2
                act.wait_ge(w_landed[p], run(i, 8 * per, 16 * (u // 2 + 1)))
                if u >= 2:
                    act.wait_ge(unit_done, run(i, per, u - 1))
                round_parts(u, parts_of(u), True)

            def round_parts(u, parts, last):
                p = u % 2
                for part, g in parts:
                    ins = nc.scalar.activation(w_hi[p][:, part], w_raw[p][:, part], ACT.Copy,
                                               scale=1.0 if g is None else g)
                if last:
                    ins.then_inc(w_rounded, 1)

            def round_piece(u, n, i, per):
                if n == 0:
                    act.wait_ge(w_landed[u % 2], run(i, 8 * per, 16 * (u // 2 + 1)))
                    act.wait_ge(unit_done, run(i, per, u - 1))
                round_parts(u, parts_of(u)[2 * n:2 * n + 2], n == 3)

            def rstd(stat, out, width, ready):
                order.link(nc.scalar.activation(out, stat, ACT.Ln, bias=eps_t[:], scale=1.0 / width))
                nc.scalar.activation(out, out, ACT.Exp, scale=-0.5).then_inc(ready, 1)

            def post_norm(t):
                for m in range(KC):
                    act.wait_ge(y_copied, KC * (t - 1) + m + 1)
                    if m >= 3:
                        act.wait_ge(yacc_done, 6 * (t - 1) + m - 2)
                    dst = work[:, ACC if m == 0 else 1 + m % 2, :]
                    nc.scalar.activation(dst, y[:, m, :], ACT.Square).then_inc(ysq_done, 1)
                if LAST_ROWS[t] + 2 < UNITS:
                    round_unit(LAST_ROWS[t] + 2)
                nc.scalar.preload_act_table_set("natural_log_exp_and_others")
                act.wait_ge(ystat_done, t)
                rstd(bank[0][:], work[:, RQ, :], D, yr_ready)

            def pre_norm(t):
                for m in range(KC):
                    if t == 0:
                        act.wait_ge(h_loaded[m // 4], 16)
                    else:
                        act.wait_ge(h_ready, KC * (t - 1) + m + 1)
                    scale = 1.0 if PRE_GAIN[t] is None else gain(PRE_GAIN[t] + m)
                    nc.scalar.activation(x_hi[:, m, :], h[:, m, :], ACT.Copy, scale=scale).then_inc(xhi_done, 1)
                    if m >= 3:
                        act.wait_ge(xacc_done, 7 * t + m - 2)
                    dst = work[:, ACC if m == 0 else 1 + m % 2, :]
                    nc.scalar.activation(dst, h[:, m, :], ACT.Square).then_inc(xsq_done, 1)
                round_unit(LAST_ROWS[t] + 3 if t else 2)
                act.wait_ge(xstat_done, t + 1)
                rstd(bank[3][:], r_pre[:], D, xr_ready)

            def ffn(u0, ev, n, sil):
                def pair(l, i=None, first=False):
                    act.wait_ge(evac, run(i, 4, ev + l + 1))
                    for m in range(2):
                        nc.scalar.activation(work[:, 2 + m, :], work[:, m, :], ACT.Silu).then_inc(silu_done, 1)
                    if not first:
                        round_unit(u0 + l + 2, i, 4)
                    for m in range(2):
                        act.wait_ge(fff_ready, run(i, 4, sil + l + m + 1))
                        c = l + m if i is None else 4 * i + (l + m)
                        nc.scalar.activation(ff_hi[:, c, :], work[:, 4 + m, :], ACT.Copy).then_inc(ffhi_done, 1)
                    round_unit(u0 + l + 3, i, 4)

                nc.scalar.preload_act_table(ACT.Silu)
                pair(0, first=True)
                with act.Fori(0, (FC - 2) // 4) as i:
                    pair(2, i)
                    pair(4, i)

            def down(u0):
                with act.Fori(0, 4) as i:
                    for l in range(2):
                        round_unit(u0 + l + 2, i, 2)
                for l in (8, 9):
                    if u0 + l + 2 < UNITS:
                        round_unit(u0 + l + 2)

            act.dma_start(par_s[:], par).then_inc(par_loaded, 16)
            for n in range(2):
                part = slice(4 * n, 4 * n + 4)
                act.dma_start(h[:, part, :], x_t[part].rearrange("m p s -> p m s")).then_inc(h_loaded[n], 16)
            act.dma_start(ident[:], ident_c).then_inc(tables_loaded, 16)
            act.dma_start(zr[:], zr_c).then_inc(tables_loaded, 16)
            act.dma_start(mask_f[:], masks).then_inc(tables_loaded, 16)
            act.dma_start(rel_s[0:33, :], rel).then_inc(tables_loaded, 16)
            act.dma_start(onehot_s[0:33, :], onehot).then_inc(tables_loaded, 16)
            act.dma_start(pos_i[:], pos.to_broadcast([P, S])).then_inc(tables_loaded, 16)
            act.wait_ge(par_loaded, 16)
            act.wait_ge(consts_ready, 2)
            round_unit(0)
            round_unit(1)
            pre_norm(0)
            for l in range(12):
                if l == 5:
                    for n, dst in enumerate((sin_t, cos_t)):
                        act.wait_ge(angle_ready, n + 1)
                        nc.scalar.activation(dst[:], (work[:, 4, :], work[:, 5, :])[n], ACT.Sin).then_inc(trig_done, 1)
                if l % 3 == 2:
                    for m in range(2):
                        b = 2 * (l // 3) + m
                        act.wait_ge(mixf_ready, b + 1)
                        nc.scalar.activation(mix_hi[:, b, :], cg[:, m, :], ACT.Copy).then_inc(mixhi_done, 1)
                if l:
                    round_unit(l + 2)
            for l in range(3):
                round_unit(CONV_OUT + l + 2)
            post_norm(1)
            pre_norm(1)
            ffn(FFN_A, EV_FFN_A, 0, 0)
            down(DOWN_A)
            post_norm(2)
            pre_norm(2)

            def attend(pair, name, i):
                def cnt(per, n):
                    return pair_count(i, pair, per, n)

                if name[0] == "S":
                    it = int(name[1])
                    if it == 0:
                        act.wait_ge(at_out, cnt(2, 1))
                    for a in range(2):
                        act.wait_ge(at_scores, cnt(16, 2 * it + a + 1))
                        lo = P if it == 0 else 0
                        src = score_bank(i, it, a)[:, lo:256]
                        if it < 4:
                            act.wait_ge(at_negmax, cnt(12, 2 * it + a + 1))
                            nc.scalar.activation(p0[:, a, it, lo:256], src, ACT.Exp,
                                                 bias=nm0[:, 2 * it + a:2 * it + a + 1]).then_inc(at_exp, 1)
                        else:
                            act.wait_ge(at_negmax, cnt(12, 8 + it - 3))
                            if it > 4:
                                act.wait_ge(at_trans, cnt(16, 2 * (it - 5) + a + 1))
                            n = 2 * (it - 4) + a
                            nc.scalar.activation(pq[:, a, :], src, ACT.Exp, bias=nm[:, n:n + 1]).then_inc(at_exp, 1)
                elif name == "FACTOR":
                    act.wait_ge(at_diff, cnt(1, 1))
                    nc.scalar.activation(c0, cdiff, ACT.Exp).then_inc(at_c0, 1)
                elif name == "V3":
                    for a in range(2):
                        act.wait_ge(at_av, cnt(16, 15 + a))
                        l_rows = slice(HD, P) if a == 0 else slice(0, HD)
                        o_rows = slice(0, HD) if a == 0 else slice(HD, P)
                        nc.scalar.activation(ln_l[o_rows, a, :], bank[6 + a][l_rows, :], ACT.Ln).then_inc(at_rl, 1)
                        act.wait_ge(at_rl, cnt(4, 2 * a + 1))
                        nc.scalar.activation(ln_l[o_rows, a, :], ln_l[o_rows, a, :], ACT.Exp,
                                             scale=-1.0).then_inc(at_rl, 1)

            def move_qk(i, group):
                act.wait_ge(rope_done, run(i, 6, 6 * group + 6))
                for half in range(2):
                    for j in range(4):
                        at = 64 * (j % 2) + 32 * half
                        act.dma_start(qk[at:at + 32, j // 2::2, :],
                                      qk_next[32 * j:32 * j + 32, half::2, :]).then_inc(qk_moved, 16)

            nc.scalar.preload_act_table_set("natural_log_exp_and_others")
            for lam in range(1, 8):
                round_unit(QKV + lam + 2)
            move_qk(None, 0)
            with act.Fori(0, 3) as i:
                u0 = QKV + GROUP
                round_unit(u0, i, GROUP)
                for kind, x, step in interleaved(6, 16):
                    if kind == "step":
                        attend(x, step, i)
                    elif kind == "chunk" and step < 4:
                        round_piece(u0 + x + 1, step, i, GROUP)
                round_unit(u0 + 7, i, GROUP)
                move_qk(i, 1)
                for lam in (8, 9):
                    round_unit(u0 + lam, i, GROUP)
            def mix_hi_block(b):
                act.wait_ge(at_out, 2 * b + 3)
                nc.scalar.activation(mix_hi[:, b, :], o_t[:, b, :], ACT.Copy).then_inc(mixhi_done, 1)

            act.wait_ge(qk_moved, MOVE * 4)
            for n, (pair, names) in enumerate(GROUP_STEPS):
                for name in names:
                    attend(pair, name, None)
                if 1 <= n < 7:
                    mix_hi_block(n - 1)
                elif n in (8, 11):
                    round_unit(ATT_OUT + (n == 11))
            for b in (6, 7):
                mix_hi_block(b)
            for l in range(3):
                round_unit(ATT_OUT + l + 2)
            post_norm(3)
            pre_norm(3)
            ffn(FFN_B, EV_FFN_B, 1, FC)
            down(DOWN_B)
            post_norm(4)
            pre_norm(4)

            shared_taps = [(b, tap) for b in range(2) for tap in range(TAPS2)]

            def make_taps(n):
                for b, tap in [shared_taps.pop(0) for _ in range(min(n, len(shared_taps)))]:
                    act.wait_ge(gated, b + 1)
                    w = par2_s[:, CDW + tap * CB + b:CDW + tap * CB + b + 1]
                    src = u2[:, b, tap:tap + S]
                    if tap == 0:
                        nc.scalar.activation(c2[:, b, :], src, ACT.Identity, scale=w,
                                             bias=par2_s[:, CDB + b:CDB + b + 1]).then_inc(tap_made, 1)
                    else:
                        if tap > 2 or b:
                            act.wait_ge(tap_added, (TAPS2 - 1) * b + tap - 2 if tap > 2 else (TAPS2 - 1) * b)
                        nc.scalar.activation(tap_out[tap % 2][:], src, ACT.Copy, scale=w).then_inc(tap_made, 1)

            act.wait_ge(par2_loaded, 16)
            for l in range(7):
                if l in (1, 3):
                    for m in range(2):
                        act.wait_ge(evac, EV_IN2 + l + 1)
                        nc.scalar.activation(work[:, 4 + m, :], work[:, 2 + m, :], ACT.Sigmoid).then_inc(sig_done, 1)
                if l:
                    round_unit(IN2 + l + 2)
                if l >= 1:
                    make_taps(3 if l == 6 else 7)

            def exponentials(t):
                lo = P if t == 0 else 0
                act.wait_ge(b_negmax, t + 1)
                x = p2s[t % 2]
                for hh in range(8):
                    nc.scalar.activation(x[:, hh, lo:256], x[:, hh, lo:256], ACT.Exp,
                                         bias=nm2s[t % 2][:, hh:hh + 1],
                                         accum_out=l2s[t % 2][:, hh:hh + 1]).then_inc(b_exp, 1)
                nc.scalar.activation(es2s[t % 2], es2s[t % 2], ACT.Exp).then_inc(b_exp, 1)

            def tile_hi(t):
                act.wait_ge(b_av, t + 1)
                nc.scalar.activation(mix_hi[:, 0:4, t * P:(t + 1) * P],
                                     bank[6 + t % 2][:].rearrange("p (b c) -> p b c", b=4),
                                     ACT.Copy).then_inc(mixhi_done, 1)

            exponentials(0)
            for t in range(4):
                lo = P if t == 0 else 0
                act.wait_ge(rl2_ready, t + 1)
                x = p2s[t % 2]
                for hh in range(8):
                    act.wait_ge(b_exp, 9 * t + hh + 1)
                    nc.scalar.activation(x[:, hh, lo:256], x[:, hh, lo:256], ACT.Copy,
                                         scale=rl2[:, hh:hh + 1]).then_inc(b_prob, 1)
                if t < 3:
                    exponentials(t + 1)
                if t:
                    tile_hi(t - 1)
                make_taps(8)
            act.wait_ge(ln_sum, 1)
            nc.scalar.activation(work[:, 4, :], bank[0][:], ACT.Copy, scale=1.0 / C2).then_inc(ln_mean, 1)
            for b in range(CB):
                act.wait_ge(ln_cent, b + 1)
                nc.scalar.activation(ln_squares[:, 2 * b:2 * b + 2, :].rearrange("p a n -> p (a n)"),
                                     c2[:, b, :], ACT.Square).then_inc(ln_sq, 1)
            tile_hi(3)
            nc.scalar.preload_act_table_set("natural_log_exp_and_others")
            act.wait_ge(ln_var, 1)
            rstd(bank[1][:], work[:, 5, :], C2, ln_r)
            for b in range(CB):
                act.wait_ge(ln_scaled, b + 1)
                nc.scalar.activation(c2[:, b, :], c2[:, b, :], ACT.Silu, bias=par2_s[:, LNB + b:LNB + b + 1],
                                     scale=par2_s[:, LNG + b:LNG + b + 1]).then_inc(z_done, 1)
                act.wait_ge(z_done, b + 1)
                nc.scalar.activation(x_hi[:, b, :], c2[:, b, :], ACT.Copy).then_inc(zhi_done, 1)
            for m in range(4):
                if m < 3:
                    act.wait_ge(pw_done, m + 1)
                else:
                    act.wait_ge(unit_done, PW2 + 1)
                nc.scalar.activation(mix_hi[:, 4 + m, :], bank[m][:], ACT.Copy).then_inc(mixhi_done, 1)
            round_unit(PW2 + 2)
            for l in range(3):
                round_unit(OUT2 + l + 2)
            post_norm(5)
            pre_norm(5)
            ffn(FFN_C, EV_FFN_C, 2, 2 * FC)
            down(DOWN_C)
            post_norm(6)

        @block.vector
        def _(dve):
            order = SelfOrder(dve, dve_order)
            v = nc.vector

            def rest_unit(u, i=None, per=0):
                p = u % 2
                dve.wait_ge(w_rounded, run(i, per, u + 1))
                rest_parts(u, parts_of(u), True)

            def rest_piece(u, n, i, per):
                if n == 0:
                    dve.wait_ge(w_rounded, run(i, per, u + 1))
                rest_parts(u, parts_of(u)[n:n + 1], n == 7)

            def rest_parts(u, parts, last):
                p = u % 2
                for part, g in parts:
                    hi = w_hi[p][:, part].bitcast(F32)
                    if g is None:
                        ins = v.tensor_tensor(w_lo[p][:, part], w_raw[p][:, part], hi, ALU.subtract)
                    else:
                        ins = v.scalar_tensor_tensor(w_lo[p][:, part], w_raw[p][:, part], g, hi,
                                                     ALU.mult, ALU.subtract)
                if last:
                    ins.then_inc(w_split, 1)

            def xlo(t, m):
                dve.wait_ge(xhi_done, KC * t + m + 1)
                hi = x_hi[:, m, :].bitcast(F32)
                if PRE_GAIN[t] is None:
                    ins = v.tensor_tensor(x_lo[:, m, :], h[:, m, :], hi, ALU.subtract)
                else:
                    ins = v.scalar_tensor_tensor(x_lo[:, m, :], h[:, m, :], gain(PRE_GAIN[t] + m), hi,
                                                 ALU.mult, ALU.subtract)
                ins.then_inc(x_ready, 1)

            def xadd(t, m):
                if m < 1:
                    return
                dve.wait_ge(xsq_done, KC * t + m + 1)
                if m > 1:
                    dve.wait_ge(xacc_done, 7 * t + m - 1)
                v.tensor_tensor(work[:, ACC, :], work[:, ACC, :], work[:, 1 + m % 2, :], ALU.add).then_inc(xacc_done, 1)

            def post_norm(t):
                last = LAST_ROWS[t]
                for m in range(KC):
                    if m < KC - 1:
                        dve.wait_ge(y_done, 7 * (t - 1) + m + 1)
                    else:
                        dve.wait_ge(unit_done, last + 1)
                    v.tensor_copy(y[:, m, :], bank[m][:]).then_inc(y_copied, 1)
                    if m >= 2:
                        dve.wait_ge(ysq_done, KC * (t - 1) + m)
                        if m > 2:
                            dve.wait_ge(yacc_done, 6 * (t - 1) + m - 2)
                        v.tensor_tensor(work[:, ACC, :], work[:, ACC, :], work[:, 1 + (m - 1) % 2, :],
                                        ALU.add).then_inc(yacc_done, 1)
                if last + 2 < UNITS:
                    rest_unit(last + 1)
                    rest_unit(last + 2)
                dve.wait_ge(yr_ready, t)

            def residual(t, m):
                order.mark(v.scalar_tensor_tensor(work[:, TMP + m % 2, :], y[:, m, :], gain(POST_GAIN[t] + m),
                                                  work[:, RQ, :], ALU.mult, ALU.mult))
                if t < 6 and m == 1:
                    xlo(t, 0)
                order.wait()
                v.tensor_tensor(h[:, m, :], h[:, m, :], work[:, TMP + m % 2, :], ALU.add).then_inc(h_ready, 1)

            def transition(t):
                if t:
                    post_norm(t)
                for m in range(KC):
                    if t:
                        residual(t, m)
                    if t < 6 and m >= (2 if t else 1):
                        xlo(t, m - 1)
                    if t < 6 and m >= 2:
                        xadd(t, m - 2)
                if t < 6:
                    xlo(t, KC - 1)
                    xadd(t, KC - 2)
                    xadd(t, KC - 1)
                    rest_unit(LAST_ROWS[t] + 3 if t else 2)

            def scaled(dst, src, r=None):
                return v.tensor_tensor(dst, src, r_pre[:] if r is None else r, ALU.mult)

            def banks_of(l):
                n = 2 * ((l + 2) % 4)
                return bank[n], bank[n + 1]

            def ffn(u0, ev, t, sil):
                def pair(l, i=None, first=False):
                    dve.wait_ge(unit_done, run(i, 4, u0 + l + 1))
                    b = banks_of(l)
                    scaled(work[:, 0, :], b[0][:])
                    scaled(work[:, 1, :], b[1][:]).then_inc(evac, 1)
                    if not first:
                        rest_unit(u0 + l + 2, i, 4)
                    dve.wait_ge(unit_done, run(i, 4, u0 + l + 2))
                    b = banks_of(l + 1)
                    order.mark(scaled(work[:, 4, :], b[0][:]))
                    scaled(work[:, 5, :], b[1][:]).then_inc(evac, 1)
                    dve.wait_ge(silu_done, run(i, 4, sil + l + 2))
                    order.wait()
                    v.tensor_tensor(work[:, 4, :], work[:, 4, :], work[:, 2, :], ALU.mult).then_inc(fff_ready, 1)
                    dve.wait_ge(evac, run(i, 4, ev + l + 2))
                    v.tensor_tensor(work[:, 5, :], work[:, 5, :], work[:, 3, :], ALU.mult).then_inc(fff_ready, 1)
                    rest_unit(u0 + l + 3, i, 4)
                    for m in range(2):
                        dve.wait_ge(ffhi_done, run(i, 4, sil + l + m + 1))
                        c = l + m if i is None else 4 * i + (l + m)
                        v.tensor_tensor(ff_lo[:, c, :], work[:, 4 + m, :], ff_hi[:, c, :].bitcast(F32),
                                        ALU.subtract).then_inc(ff_ready, 1)

                dve.wait_ge(xr_ready, t + 1)
                pair(0, first=True)
                with dve.Fori(0, (FC - 2) // 4) as i:
                    order.enter(i, 2)
                    pair(2, i)
                    pair(4, i)
                order.leave((FC - 2) // 4)

            def down(u0):
                with dve.Fori(0, 4) as i:
                    for l in range(2):
                        rest_unit(u0 + l + 2, i, 2)
                rest_unit(u0 + 10)

            dve.wait_ge(par_loaded, 16)
            rest_unit(0)
            rest_unit(1)
            for n in range(2):
                dve.wait_ge(h_loaded[n], 16)
            transition(0)
            dve.wait_ge(tables_loaded, 16 * 6)
            v.tensor_copy(mask_b[:], mask_f[:]).then_inc(casts_ready, 1)
            v.tensor_copy(ident_b[:], ident[:]).then_inc(casts_ready, 1)
            dve.wait_ge(b_row, 1)
            v.tensor_copy(erow[0:8, :], bank[2][0:8, 0:384]).then_inc(b_rowcopied, 1)
            def rotary_angles():
                order.link(v.tensor_copy(work[:, 3, :], pos_i[:]))
                order.link(v.tensor_scalar(ang[:], work[:, 3, :], gain(INV_FREQ), None, ALU.mult))
                for n in range(2):
                    r = work[:, 4 + n, :]
                    order.link(v.tensor_scalar(turn[:], ang[:], 1.0 / (2 * math.pi), 0.25 * n, ALU.mult, ALU.add))
                    src = ang[:]
                    for part in (TWO_PI_1, TWO_PI_2, TWO_PI_3):
                        order.link(v.scalar_tensor_tensor(r, turn[:], -part, src, ALU.mult, ALU.add))
                        src = r
                    order.link(v.tensor_scalar(r, r, 0.5 * math.pi * n, PI_CLAMP, ALU.add, ALU.min))
                    v.tensor_scalar(r, r, -PI_CLAMP, None, ALU.max).then_inc(angle_ready, 1)

            order.link(v.memset(u1[:, :, 0:2], 0.0))
            dve.wait_ge(xr_ready, 1)
            for l in range(12):
                if l == 4:
                    rotary_angles()
                g3 = l // 3
                dve.wait_ge(unit_done, l + 1)
                b = banks_of(l)
                if l % 3 == 0:
                    if l == 0:
                        order.link(v.tensor_tensor(work[:, 2, :], r_pre[:], r_pre[:], ALU.mult))
                    for m in range(2):
                        ins = scaled(work[:, m, :], b[m][:], work[:, 2, :])
                        if m:
                            ins.then_inc(evac, 1)
                        else:
                            order.mark(ins)
                elif l % 3 == 1:
                    dve.wait_ge(evac, l)
                    for m in range(2):
                        ins = scaled(u1[:, m, 2:S + 2], b[m][:], work[:, m, :])
                        if m:
                            ins.then_inc(evac, 1)
                        else:
                            order.mark(ins)
                    dve.wait_ge(evac, l + 1)
                    order.wait()
                    for tap in range(TAPS1):
                        for m in range(2):
                            w = gain(CONVW + tap * KC + 2 * g3 + m)
                            src = u1[:, m, tap:tap + S]
                            if tap == 0:
                                ins = v.tensor_scalar(cv[:, m, :], src, w, None, ALU.mult)
                            else:
                                order.wait(1)
                                ins = v.scalar_tensor_tensor(cv[:, m, :], src, w, cv[:, m, :], ALU.mult, ALU.add)
                            order.mark(ins)
                else:
                    if g3:
                        dve.wait_ge(mixhi_done, 2 * g3)
                    for m in range(2):
                        ins = scaled(cg[:, m, :], b[m][:])
                        if m:
                            ins.then_inc(evac, 1)
                        else:
                            order.mark(ins)
                    order.wait()
                    dve.wait_ge(evac, l + 1)
                    for m in range(2):
                        v.tensor_tensor(cg[:, m, :], cg[:, m, :], cv[:, m, :], ALU.mult).then_inc(mixf_ready, 1)
                    for m in range(2):
                        c = 2 * g3 + m
                        dve.wait_ge(mixhi_done, c + 1)
                        v.tensor_tensor(mix_lo[:, c, :], cg[:, m, :], mix_hi[:, c, :].bitcast(F32),
                                        ALU.subtract).then_inc(mix_ready, 1)
                if l:
                    rest_unit(l + 2)
            for l in range(2):
                rest_unit(CONV_OUT + l + 2)
            dve.wait_ge(trig_done, 2)
            dve.wait_ge(skew_written, 16)
            transition(1)
            ffn(FFN_A, EV_FFN_A, 1, 0)
            down(DOWN_A)
            transition(2)

            dve.wait_ge(xr_ready, 3)
            v.tensor_tensor(cos_t[:], cos_t[:], r_pre[:], ALU.mult)
            order.mark(v.tensor_tensor(sin_t[:], sin_t[:], r_pre[:], ALU.mult))
            dve.wait_ge(rcol_ps, 1)
            v.tensor_copy(r_col[:], bank[2][:, 0:8]).then_inc(rcol_ready, 1)
            v.memset(cm, 0.0).then_inc(at_out, 1)
            for b in range(3):
                order.mark(v.memset(v1s[b][:, :, :, HD:2 * HD], 1.0))
            order.wait()
            dve.wait_ge(rcol_ready, 1)

            def rotate_first(lam, b, i, group):
                f = 1.0 if lam % 2 else HD ** -0.5
                if group or lam:
                    dve.wait_ge(rope_done, run(i, 6, 6 * group + lam))
                v.scalar_tensor_tensor(turned[:, 0, :], b[0][:], f, cos_t[:], ALU.mult, ALU.mult)
                return v.scalar_tensor_tensor(turned[:, 3, :], b[0][:], f, sin_t[:], ALU.mult, ALU.mult)

            def rotate_second(lam, b, i, group):
                br, is_k = lam // 2, lam % 2
                f = 1.0 if is_k else HD ** -0.5
                dst = [qk_next[:, 4 * br + 2 * is_k + n, :] for n in range(2)]
                if br:
                    dst = [d.rearrange("p (r n) -> p n r", r=4) for d in dst]

                def seen(slot):
                    t_ = turned[:, slot, :]
                    return t_.rearrange("p (n r) -> p n r", r=4) if br else t_

                v.scalar_tensor_tensor(turned[:, 1, :], b[1][:], f, sin_t[:], ALU.mult, ALU.mult)
                v.scalar_tensor_tensor(turned[:, 2, :], b[1][:], f, cos_t[:], ALU.mult, ALU.mult).then_inc(evac, 1)
                dve.wait_ge(evac, run(i, 9, EV_QKV + 9 * group + lam + 1))
                v.tensor_tensor(dst[0], seen(0), seen(1), ALU.subtract)
                v.tensor_tensor(dst[1], seen(2), seen(3), ALU.add).then_inc(rope_done, 1)

            def take_v(lam, b):
                br = lam - 6
                for t in range(4):
                    src = b[t // 2][:, (t % 2) * 256:(t % 2) * 256 + 256]
                    src = src.rearrange("p (a c d) -> p a c d", a=2, c=2)
                    col = r_col[:, (4 if br == 0 else 0) + t:(4 if br == 0 else 0) + t + 1]
                    dst = v1s[br][:, t, :, :].rearrange("p a (c d) -> p a c d", c=3)[:, :, 0:3:2, :]
                    ins = v.tensor_scalar(dst, src, col, None, ALU.mult)
                ins.then_inc(evac, 1)

            def attend(pair, name, i):
                def cnt(per, n):
                    return pair_count(i, pair, per, n)

                if name[0] == "S" and int(name[1]) < 4:
                    it = int(name[1])
                    lo = P if it == 0 else 0
                    for a in range(2):
                        dve.wait_ge(at_scores, cnt(16, 2 * it + a + 1))
                        v.tensor_reduce(nm0[:, 2 * it + a:2 * it + a + 1], score_bank(i, it, a)[:, lo:256],
                                        AX.X, ALU.max, negate=True).then_inc(at_negmax, 1)
                elif name[0] == "S":
                    it = int(name[1])
                    n = 2 * (it - 4)
                    for a in range(2):
                        dve.wait_ge(at_scores, cnt(16, 2 * it + a + 1))
                        ins = v.tensor_reduce(nm[:, n + a:n + a + 1], score_bank(i, it, a)[:, 0:256],
                                              AX.X, ALU.max, negate=True)
                    order.link(ins)
                    v.tensor_tensor(nm[:, n:n + 2], nm[:, n:n + 2], nm0r[:, n:n + 2],
                                    ALU.min).then_inc(at_negmax, 1)
                    if it == 7:
                        dve.wait_ge(at_negmax, cnt(12, 12))
                        v.tensor_tensor(cdiff, nm, nm0r, ALU.subtract).then_inc(at_diff, 1)
                elif name == "MAXPERM":
                    dve.wait_ge(at_perm, cnt(2, 1))
                    order.link(v.tensor_copy(nm0r, bank[4][:, 0:8]))
                elif name[0] == "T":
                    it = int(name[1])
                    k = ITEM_ORDER[it]
                    lo = P if it == 0 else 0
                    for a in range(2):
                        dve.wait_ge(at_trans, cnt(16, 2 * k + a + 1))
                        if k:
                            dve.wait_ge(at_av, cnt(16, 2 * (k - 1) + a + 1))
                        if it < 4:
                            c = (256 - lo) // P
                            src = bank[4 + a][:, lo:256].rearrange("p (c i r) -> p c r i", c=c, r=4)
                            dst = pt[:, a, lo:256].rearrange("p (c r i) -> p c r i", c=c, r=4)
                            if c == 1:
                                v.tensor_copy(dst[:, 0], src[:, 0]).then_inc(at_ptcopy, 1)
                            else:
                                v.tensor_copy(dst, src).then_inc(at_ptcopy, 1)
                        else:
                            v.tensor_copy(pt[:, a, :], bank[4 + a][:, 0:256]).then_inc(at_ptcopy, 1)
                elif name == "FACTOR":
                    dve.wait_ge(at_c0, cnt(1, 1))
                    for j in range(4):
                        rows = slice(32 * j, 32 * j + 32)
                        dst = cm[rows, :].rearrange("p (r j a) -> p r j a", r=4, j=4)[:, :, j, :]
                        ins = v.tensor_copy(dst, c0[rows, :].rearrange("p (r a) -> p r a", r=4))
                    ins.then_inc(at_cm, 1)
                elif name == "FACTORPERM":
                    dve.wait_ge(at_perm, cnt(2, 2))
                    order.link(v.tensor_copy(c0n, bank[5][:, 0:8]))
                    for t in range(4):
                        lo = P if t == 0 else 0
                        for a in range(2):
                            dve.wait_ge(at_exp, cnt(16, 2 * t + a + 1))
                            v.tensor_scalar(p0[:, a, t, lo:256], p0[:, a, t, lo:256],
                                            c0n[:, 2 * t + a:2 * t + a + 1], None, ALU.mult).then_inc(at_scaled, 1)
                elif name == "OUT":
                    for a in range(2):
                        dve.wait_ge(at_rl, cnt(4, 2 * a + 2))
                        rows = slice(0, HD) if a == 0 else slice(HD, P)
                        blk = 6 + pair if i is None else 2 * i + pair
                        dst = o_t[rows, blk, :].rearrange("p (n r) -> p r n", r=4)
                        v.tensor_tensor(dst, bank[6 + a][rows, :].rearrange("p (r n) -> p r n", r=4),
                                        ln_l[rows, a, :].rearrange("p (r n) -> p r n", r=4),
                                        ALU.mult).then_inc(at_out, 1)

            for lam in range(GROUP):
                dve.wait_ge(unit_done, QKV + lam + 1)
                if lam < 6:
                    rotate_first(lam, banks_of(lam), None, 0)
                    rotate_second(lam, banks_of(lam), None, 0)
                elif lam < 8:
                    take_v(lam, v_banks(lam))
                if 1 <= lam <= 7:
                    rest_unit(QKV + lam + 2)
            with dve.Fori(0, 3) as i:
                order.enter(i, 2 * 6)
                u0 = QKV + GROUP
                rest_unit(u0, i, GROUP)
                dve.wait_ge(unit_done, run(i, GROUP, u0))
                take_v(8, v_banks(8))
                for kind, x, step in interleaved(6, 16):
                    if kind == "step":
                        attend(x, step, i)
                    elif kind == "half_end":
                        dve.wait_ge(half_done, run(i, 6, x + 1))
                        rotate_first(x, (bank[2], bank[3]), i, 1).then_inc(half_read, 1)
                    elif kind == "unit_end":
                        dve.wait_ge(unit_done, run(i, GROUP, u0 + x + 1))
                        if x == 0:
                            dve.wait_ge(qk_moved, run(i, MOVE, MOVE))
                        rotate_second(x, (bank[2], bank[3]), i, 1)
                    elif kind == "chunk" and 4 <= step < 12:
                        rest_piece(u0 + x + 1, step - 4, i, GROUP)
                rest_unit(u0 + 7, i, GROUP)
                for lam in (6, 7):
                    dve.wait_ge(unit_done, run(i, GROUP, u0 + lam + 1))
                    take_v(lam, v_banks(lam))
                    rest_unit(u0 + lam + 2, i, GROUP)
            order.leave(3)
            dve.wait_ge(unit_done, ATT_OUT)
            take_v(8, v_banks(8))
            def mix_lo_block(b):
                dve.wait_ge(mixhi_done, KC + b + 1)
                v.tensor_tensor(mix_lo[:, b, :], o_t[:, b, :], mix_hi[:, b, :].bitcast(F32),
                                ALU.subtract).then_inc(mix_ready, 1)

            for n, (pair, names) in enumerate(GROUP_STEPS):
                for name in names:
                    attend(pair, name, None)
                if 1 <= n < 7:
                    mix_lo_block(n - 1)
                elif n in (8, 11):
                    rest_unit(ATT_OUT + (n == 11))
            for b in (6, 7):
                mix_lo_block(b)
            for l in range(2):
                rest_unit(ATT_OUT + l + 2)
            transition(3)
            ffn(FFN_B, EV_FFN_B, 3, FC)
            down(DOWN_B)
            transition(4)

            order.mark(v.memset(u2[:, :, 0:TAPS2 - 1], 0.0))
            dve.wait_ge(par2_loaded, 16)
            order.mark(v.tensor_scalar(nsink, par2_s[:, SINK:SINK + 8], -1.0, None, ALU.mult))
            order.wait()
            dve.wait_ge(xr_ready, 5)
            taps = [(tap, 2 + b) for tap in range(TAPS2) for b in range(2)]

            def conv_taps(n):
                for tap, b in [taps.pop(0) for _ in range(min(n, len(taps)))]:
                    w = par2_s[:, CDW + tap * CB + b:CDW + tap * CB + b + 1]
                    src = u2[:, b, tap:tap + S]
                    if tap == 0:
                        ins = v.tensor_scalar(c2[:, b, :], src, w, par2_s[:, CDB + b:CDB + b + 1], ALU.mult, ALU.add)
                    else:
                        order.wait(1)
                        ins = v.scalar_tensor_tensor(c2[:, b, :], src, w, c2[:, b, :], ALU.mult, ALU.add)
                    order.mark(ins)

            for l in range(7):
                dve.wait_ge(unit_done, IN2 + l + 1)
                b = banks_of(l)
                if l in (0, 2):
                    if l:
                        dve.wait_ge(gated, 2)
                    order.mark(scaled(work[:, 0, :], b[0][:]))
                    scaled(work[:, 1, :], b[1][:]).then_inc(evac, 1)
                elif l in (1, 3):
                    scaled(work[:, 2, :], b[0][:])
                    scaled(work[:, 3, :], b[1][:]).then_inc(evac, 1)
                    dve.wait_ge(evac, EV_IN2 + l)
                    order.wait()
                    for m in range(2):
                        dve.wait_ge(sig_done, l + m)
                        ins = v.tensor_tensor(u2[:, l - 1 + m, TAPS2 - 1:TAPS2 - 1 + S], work[:, m, :],
                                              work[:, 4 + m, :], ALU.mult)
                        if l == 1:
                            ins.then_inc(gated, 1)
                        else:
                            order.mark(ins)
                elif l in (4, 5):
                    order.mark(scaled(q2[:, 2 * (l - 4), :], b[0][:]))
                    scaled(q2[:, 2 * (l - 4) + 1, :], b[1][:]).then_inc(evac, 1)
                else:
                    dve.wait_ge(rcol_ps, 2)
                    v.tensor_copy(r_col[:, 0:4], bank[2][:, 0:4]).then_inc(rcol_ready, 1)
                    order.mark(scaled(k2[:], b[0][:]))
                    dve.wait_ge(rcol_ready, 2)
                    for t in range(4):
                        ins = v.tensor_scalar(v2[:, t, :], b[1][:, t * P:(t + 1) * P], r_col[:, t:t + 1], None, ALU.mult)
                    ins.then_inc(evac, 1)
                if 1 <= l < 6:
                    rest_unit(IN2 + l + 2)
                if 3 <= l < 6:
                    order.wait()
                    conv_taps(11)

            def logits(t):
                lo = P if t == 0 else 0
                x, nm2 = p2s[t % 2], nm2s[t % 2]
                dve.wait_ge(b_scores, t + 1)
                for n in range(4):
                    ins = v.scalar_tensor_tensor(x[:, 2 * n:2 * n + 2, lo:256],
                                                 bank[n][:].rearrange("p (h k) -> p h k", h=2)[:, :, lo:256],
                                                 HD ** -0.5, bias2[:, 2 * n:2 * n + 2, lo:256], ALU.mult, ALU.add)
                ins.then_inc(b_logits, 1)
                dve.wait_ge(b_logits, t + 1)
                order.link(v.tensor_reduce(nm2, x[:, :, lo:256], AX.X, ALU.max, negate=True))
                order.link(v.tensor_tensor(nm2, nm2, nsink, ALU.min))
                v.tensor_tensor(es2s[t % 2], par2_s[:, SINK:SINK + 8], nm2, ALU.add).then_inc(b_negmax, 1)

            def tile_lo(t):
                dve.wait_ge(mixhi_done, 2 * KC + t + 1)
                cols = slice(t * P, (t + 1) * P)
                v.tensor_tensor(mix_lo[:, 0:4, cols], bank[6 + t % 2][:].rearrange("p (b c) -> p b c", b=4),
                                mix_hi[:, 0:4, cols].bitcast(F32), ALU.subtract).then_inc(mix_ready, 1)

            dve.wait_ge(bias_loaded, 16 * 8)
            logits(0)
            rest_unit(IN2 + 8)
            conv_taps(5)
            for t in range(4):
                lo = P if t == 0 else 0
                dve.wait_ge(b_exp, 9 * t + 9)
                if t:
                    dve.wait_ge(b_prob, 8 * t)
                order.link(v.tensor_tensor(l2s[t % 2], l2s[t % 2], es2s[t % 2], ALU.add))
                v.reciprocal(rl2, l2s[t % 2]).then_inc(rl2_ready, 1)
                if t < 3:
                    logits(t + 1)
                    conv_taps(5)
                else:
                    dve.wait_ge(tap_added, 2 * (TAPS2 - 1))
                    dve.wait_ge(ln_mean, 1)
                    for b in range(CB):
                        v.tensor_tensor(c2[:, b, :], c2[:, b, :], work[:, 4, :], ALU.subtract).then_inc(ln_cent, 1)
                if t:
                    tile_lo(t - 1)
                for rd in range(2):
                    dve.wait_ge(b_trans, 2 * t + rd + 1)
                    if t:
                        dve.wait_ge(b_av, t)
                    for n in range(2):
                        dst = pt2[:, 2 * rd + n, :].rearrange("p (h k) -> p h k", h=2)[:, :, lo:256]
                        v.tensor_copy(dst, bank[4 + n][:].rearrange("p (h k) -> p h k", h=2)[:, :, lo:256])\
                            .then_inc(b_ptcopy, 1)
                conv_taps(3)
                if t == 2:
                    assert not taps
                    order.wait()
                    v.tensor_copy(st[:, 64:65], st[:, 0:1]).then_inc(conv_ready, 1)
            tile_lo(3)

            dve.wait_ge(ln_r, 1)
            for b in range(CB):
                dve.wait_ge(ln_cent, b + 1)
                dve.wait_ge(ln_sq, b + 1)
                v.tensor_tensor(c2[:, b, :], c2[:, b, :], work[:, 5, :], ALU.mult).then_inc(ln_scaled, 1)
            for b in range(CB):
                dve.wait_ge(zhi_done, b + 1)
                v.tensor_tensor(x_lo[:, b, :], c2[:, b, :], x_hi[:, b, :].bitcast(F32), ALU.subtract).then_inc(z_ready, 1)
            for m in range(4):
                dve.wait_ge(mixhi_done, 2 * KC + 4 + m + 1)
                v.tensor_tensor(mix_lo[:, 4 + m, :], bank[m][:], mix_hi[:, 4 + m, :].bitcast(F32),
                                ALU.subtract).then_inc(mix_ready, 1)
            rest_unit(PW2 + 2)
            for l in range(2):
                rest_unit(OUT2 + l + 2)
            transition(5)
            ffn(FFN_C, EV_FFN_C, 5, 2 * FC)
            down(DOWN_C)
            transition(6)

        @block.tensor
        def _(pe):
            mm = nc.tensor.matmul

            def products(out, w, hi, lo, start, stop, flip=False, **kw):
                pairs = ((w[0], hi), (w[0], lo), (w[1], hi))
                for n, (a, b) in enumerate(pairs):
                    ins = mm(out, b if flip else a, a if flip else b,
                             start=start and n == 0, stop=stop and n == 2, **kw)
                return ins

            def weights(u, at, n=P):
                return w_hi[u % 2][:, at:at + n], w_lo[u % 2][:, at:at + n]

            def block_of(u, m, b, ks, hi=None, lo=None):
                hi, lo = (x_hi, x_lo) if hi is None else (hi, lo)
                for k in ks:
                    ins = products(b[m][:], weights(u, k * 256 + m * P), hi[:, k, :], lo[:, k, :], k == 0, k == KC - 1)
                return ins

            def banks_of(l):
                n = 2 * ((l + 2) % 4)
                return bank[n], bank[n + 1]

            def unit(u, l, ev, i=None, per=0, hi=None, lo=None):
                pe.wait_ge(w_split, run(i, per, u + 1))
                if l >= 4:
                    pe.wait_ge(evac, run(i, per, ev + l - 3))
                for m in range(2):
                    ins = block_of(u, m, banks_of(l), range(KC), hi, lo)
                ins.then_inc(unit_done, 1)

            def xstat(t):
                pe.wait_ge(xacc_done, 7 * (t + 1))
                mm(bank[3][:], ones[:], work[:, 0, :], start=True, stop=True).then_inc(xstat_done, 1)

            def first_units(t, u):
                early = 5
                if t:
                    for _ in range(WARM):
                        mm(bank[1][:, 0:3 * P], ident_b[:], mask_b[:], start=True, stop=True)
                pe.wait_ge(w_split, u + 2)
                for k in range(early):
                    pe.wait_ge(x_ready, KC * t + k + 1)
                    for l in range(2):
                        for m in range(2):
                            block_of(u + l, m, banks_of(l), [k])
                for l in range(2):
                    for k in range(early, KC):
                        if l == 0:
                            pe.wait_ge(x_ready, KC * t + k + 1)
                        for m in range(2):
                            ins = block_of(u + l, m, banks_of(l), [k])
                    ins.then_inc(unit_done, 1)
                    if l == 0:
                        xstat(t)
                pe.wait_ge(xr_ready, t + 1)

            def ffn(t, u0, ev):
                first_units(t, u0)
                with pe.Fori(0, (FC - 2) // 4) as i:
                    for l in range(2, 6):
                        pe.wait_ge(w_split, run(i, 4, u0 + l + 1))
                        pe.wait_ge(evac, run(i, 4, ev + max(l - 3, 0)))
                        for m in range(2):
                            ins = block_of(u0 + l, m, banks_of(l), range(KC))
                        ins.then_inc(unit_done, 1)

            def rows(u, c, hi, lo, start=False, i=None):
                pe.wait_ge(w_split, run(i, 2, u + 1))
                for kk in range(2):
                    n = 2 * c + kk if i is None else 2 * 2 * i + (2 * c + kk)
                    for m in range(KC):
                        ins = products(bank[m][:], weights(u, kk * D + m * P), hi[:, n, :], lo[:, n, :],
                                       start and kk == 0, False)
                ins.then_inc(unit_done, 1)

            def last_rows(t, u, c, hi, lo):
                pe.wait_ge(w_split, u + 1)
                for m in range(KC):
                    for kk in range(2):
                        n = 2 * c + kk
                        ins = products(bank[m][:], weights(u, kk * D + m * P), hi[:, n, :], lo[:, n, :], False, kk == 1)
                    if m < KC - 1:
                        ins.then_inc(y_done, 1)
                    else:
                        ins.then_inc(unit_done, 1)
                pe.wait_ge(yacc_done, 6 * t)
                mm(bank[0][:], ones[:], work[:, 0, :], start=True, stop=False)
                pe.wait_ge(ysq_done, KC * t)
                mm(bank[0][:], ones[:], work[:, 2, :], start=False, stop=True).then_inc(ystat_done, 1)

            def down(t, u0, ev, base):
                pe.wait_ge(evac, ev)
                for c in range(2):
                    pe.wait_ge(ff_ready, base + 2 * c + 2)
                    rows(u0 + c, c, ff_hi, ff_lo, start=c == 0)
                with pe.Fori(0, 4) as i:
                    for c in (2, 3):
                        pe.wait_ge(ff_ready, run(i, 4, base + 2 * c + 2))
                        rows(u0 + c, c, ff_hi, ff_lo, i=i)
                pe.wait_ge(ff_ready, base + FC)
                last_rows(t, u0 + 10, 10, ff_hi, ff_lo)

            def projection(t, u0, ev, ready):
                pe.wait_ge(evac, ev)
                for c in range(4):
                    pe.wait_ge(mix_ready, ready[c])
                    if c < 3:
                        rows(u0 + c, c, mix_hi, mix_lo, start=c == 0)
                    else:
                        last_rows(t, u0 + c, c, mix_hi, mix_lo)

            pe.wait_ge(consts_ready, 2)
            first_units(0, CONV_IN)
            pe.wait_ge(tables_loaded, 16 * 6)
            mm(bank[2][0:8, 0:384], rel_s[0:33, :], onehot_s[0:33, :], start=True, stop=True).then_inc(b_row, 1)
            pe.wait_ge(casts_ready, 2)
            pe.wait_ge(b_rowcopied, 1)
            for l in range(2, 12):
                unit(CONV_IN + l, l, EV_CONV)
            projection(1, CONV_OUT, EV_FFN_A, [2, 4, 6, 8])
            ffn(1, FFN_A, EV_FFN_A)
            down(2, DOWN_A, EV_QKV, 0)

            first_units(2, QKV)
            for n in range(8):
                cols = slice(n, S, 4) if n < 4 else slice((n - 4) * P, (n - 3) * P)
                ins = mm(bank[2][:, n:n + 1], r_pre[0:1, cols], ones[0:1, 0:1], start=True, stop=True)
            ins.then_inc(rcol_ps, 1)

            def v_unit(u, lam, i=None, per=0):
                pe.wait_ge(w_split, run(i, per, u + 1))
                b = v_banks(min(lam, 8))
                first, chunks = {8: (0, KC // 2), 9: (KC // 2, KC // 2)}.get(lam, (0, KC))
                for t in range(4):
                    cols = slice(t * P, (t + 1) * P) if lam == 6 else slice(t, S, 4)
                    for n in range(chunks):
                        k = first + n
                        fresh = k == 0 and (lam < 8 or t % 2 == 0)
                        ins = products(b[t // 2][:, (t % 2) * 256:(t % 2) * 256 + 256], weights(u, n * 256, 256),
                                       x_hi[:, k, cols], x_lo[:, k, cols], fresh, k == KC - 1, flip=True,
                                       skip_group_check=lam >= 8)
                ins.then_inc(unit_done, 1)

            def attend(pair, name, i):
                def cnt(per, n):
                    return pair_count(i, pair, per, n)

                if name[0] == "S":
                    it = int(name[1])
                    t = it % 4
                    lo = P if it == 0 else 0
                    depth = 2 if i is None else 1
                    out = [score_bank(i, it, a) for a in range(2)]
                    for a in range(2):
                        if it >= depth:
                            pe.wait_ge(at_exp, cnt(16, 2 * (it - depth) + a + 1))
                        m0 = lo if it < 4 else P
                        mm(out[a][:, lo:256], ident_b[:], mask_b[:, m0:m0 + 256 - lo], start=True, stop=False)
                    parts = [(0, slice((t - 1) * P if t else 0, (t + 1) * P), slice(lo, 256))] if it < 4 else \
                        [(br, slice(t * P, (t + 1) * P), slice((br - 1) * P, br * P)) for br in (1, 2)]
                    for n, (br, keys, cols) in enumerate(parts):
                        for a in range(2):
                            rows_ = slice(HD * a, HD * a + HD)
                            last = n == len(parts) - 1
                            ins = mm(out[a][:, cols], qk[rows_, 4 * br + pair, t * P:(t + 1) * P],
                                     qk[rows_, 4 * br + 2 + pair, keys], start=False, stop=last)
                            if last:
                                ins.then_inc(at_scores, 1)
                elif name[0] == "T":
                    it = int(name[1])
                    k = ITEM_ORDER[it]
                    for a in range(2):
                        if it < 4:
                            pe.wait_ge(at_scaled, cnt(8, 2 * it + a + 1))
                            src = p0[:, a, it, :]
                        else:
                            pe.wait_ge(at_exp, cnt(16, 2 * it + a + 1))
                            src = pq[:, a, :]
                        if k:
                            pe.wait_ge(at_ptcopy, cnt(16, 2 * (k - 1) + a + 1))
                        for c in range(1 if it == 0 else 0, 2):
                            ins = nc.tensor.transpose(bank[4 + a][:, c * P:(c + 1) * P],
                                                      src[:, c * P:(c + 1) * P], ident[:])
                        ins.then_inc(at_trans, 1)
                elif name[0] == "V":
                    it = int(name[1])
                    k = ITEM_ORDER[it]
                    t = it % 4
                    if k == 0:
                        pe.wait_ge(at_out, cnt(2, 1))
                    for a in range(2):
                        pe.wait_ge(at_ptcopy, cnt(16, 2 * k + a + 1))
                        for c in range(1 if it == 0 else 0, 2):
                            br = 0 if it < 4 else 1 + c
                            tile = t - 1 + c if it < 4 else t
                            vv = v1s[br][:, tile, pair, a * HD:a * HD + P]
                            rhs = pt[:, a, c * P:(c + 1) * P]
                            if it < 4:
                                out = bank[6 + a][:].rearrange("p (r n) -> p r n", r=4)[:, :, 32 * t:32 * t + 32]
                                rhs = rhs.rearrange("p (r i) -> p r i", r=4)
                            else:
                                out = bank[6 + a][:, t * P:(t + 1) * P]
                            ins = mm(out, vv, rhs, start=k == 0 and c == 0, stop=k == 7 and c == 1,
                                     skip_group_check=True)
                        ins.then_inc(at_av, 1)
                elif name == "MAXPERM":
                    if pair == 0:
                        pe.wait_ge(evac, EV_QKV + 36 if i is None else run(i, 9, EV_QKV + 9))
                    pe.wait_ge(at_negmax, cnt(12, 8))
                    for r in range(4):
                        for j in range(4):
                            ins = mm(bank[4][32 * j:32 * j + 32, 2 * r:2 * r + 2], ident[:, r::4],
                                     nm0[:, 2 * j:2 * j + 2], start=True, stop=True)
                    ins.then_inc(at_perm, 1)
                elif name == "FACTORPERM":
                    pe.wait_ge(at_cm, cnt(1, 1))
                    for r in range(4):
                        ins = mm(bank[5][:, 0:8], zr[:, 3 - r:3 - r + P], cm[:, 8 * r:8 * r + 8],
                                 start=r == 0, stop=r == 3)
                    ins.then_inc(at_perm, 1)

            for lam in range(2, 6):
                if lam == 3:
                    pe.wait_ge(rcol_ready, 1)
                unit(QKV + lam, lam, EV_QKV)
            for lam in range(6, GROUP):
                pe.wait_ge(evac, EV_QKV + min(lam, 8) - 2)
                v_unit(QKV + lam, lam)
            with pe.Fori(0, 3) as i:
                u0 = QKV + GROUP
                pe.wait_ge(evac, run(i, 9, EV_QKV + 8))
                pe.wait_ge(qk_moved, run(i, MOVE, MOVE))
                for kind, x, step in interleaved(6, 16):
                    if kind == "step":
                        attend(x, step, i)
                    elif kind == "chunk":
                        if step == 0:
                            pe.wait_ge(w_split, run(i, GROUP, u0 + x + 1))
                            if x:
                                pe.wait_ge(half_read, run(i, 6, x))
                        elif step == KC and x:
                            pe.wait_ge(evac, run(i, 9, EV_QKV + 9 + x))
                        ins = block_of(u0 + x, step // KC, (bank[2], bank[3]), [step % KC])
                    elif kind == "half_end":
                        ins.then_inc(half_done, 1)
                    else:
                        ins.then_inc(unit_done, 1)
                pe.wait_ge(evac, run(i, 9, EV_QKV + 9 + 6))
                v_unit(u0 + 6, 6, i, GROUP)
                pe.wait_ge(at_exp, run(i, 32, 32))
                v_unit(u0 + 7, 7, i, GROUP)
                pe.wait_ge(at_ptcopy, run(i, 32, 32))
                v_unit(u0 + 8, 8, i, GROUP)
                v_unit(u0 + 9, 9, i, GROUP)
            pe.wait_ge(evac, EV_QKV + 35)
            pe.wait_ge(qk_moved, MOVE * 4)
            for pair, names in GROUP_STEPS:
                for name in names:
                    attend(pair, name, None)
            pe.wait_ge(at_out, 2 * KC + 1)
            projection(3, ATT_OUT, EV_FFN_B, [10, 12, 14, 16])
            ffn(3, FFN_B, EV_FFN_B)
            down(4, DOWN_B, EV_IN2, FC)

            first_units(4, IN2)
            for l in range(2, 6):
                unit(IN2 + l, l, EV_IN2)
            pe.wait_ge(evac, EV_IN2 + 4)
            for t in range(4):
                ins = mm(bank[2][:, t:t + 1], r_pre[0:1, t * P:(t + 1) * P], ones[0:1, 0:1], start=True, stop=True)
            ins.then_inc(rcol_ps, 1)
            u = IN2 + 6
            pe.wait_ge(w_split, u + 1)
            block_of(u, 0, banks_of(6), range(KC))
            for t in range(4):
                for k in range(KC):
                    ins = products(banks_of(6)[1][:, t * P:(t + 1) * P], weights(u, k * 256 + P),
                                   x_hi[:, k, t * P:(t + 1) * P], x_lo[:, k, t * P:(t + 1) * P],
                                   k == 0, k == KC - 1, flip=True)
            ins.then_inc(unit_done, 1)
            pe.wait_ge(evac, EV_IN2 + 7)

            def scores2(t):
                lo = P if t == 0 else 0
                if t:
                    pe.wait_ge(b_logits, t)
                for b in range(4):
                    for kv in range(2):
                        rows_ = slice(HD * kv, HD * kv + HD)
                        at = (b % 2) * 256
                        ins = mm(bank[2 * kv + b // 2][:, at + lo:at + 256], q2[rows_, b, t * P:(t + 1) * P],
                                 k2[rows_, (t - 1) * P + lo:(t + 1) * P], start=True, stop=True)
                ins.then_inc(b_scores, 1)

            scores2(0)
            scores2(1)
            for t in range(4):
                if t < 2:
                    scores2(t + 2)
                if t == 3:
                    pe.wait_ge(b_logits, 4)
                    pe.wait_ge(conv_ready, 1)
                    pe.wait_ge(tap_added, 2 * (TAPS2 - 1))
                    for b in range(CB):
                        ins = mm(bank[0][:], ones[:], c2[:, b, :], start=b == 0, stop=b == CB - 1)
                    ins.then_inc(ln_sum, 1)
                for rd in range(2):
                    if t or rd:
                        pe.wait_ge(b_ptcopy, 4 * t + 2 * rd)
                    for hh in range(4):
                        pe.wait_ge(b_prob, 8 * t + 4 * rd + hh + 1)
                        for c in range(1 if t == 0 else 0, 2):
                            ins = nc.tensor.transpose(bank[4 + hh // 2][:, (hh % 2) * 256 + c * P:(hh % 2) * 256 + c * P + P],
                                                      p2s[t % 2][:, 4 * rd + hh, c * P:(c + 1) * P], ident[:])
                    ins.then_inc(b_trans, 1)
                if t >= 2:
                    pe.wait_ge(mix_ready, 2 * KC + t - 1)
                for hh in range(8):
                    if hh % 4 == 0:
                        pe.wait_ge(b_ptcopy, 4 * t + 2 * (hh // 4) + 2)
                    kv = hh // 4
                    for c in range(1 if t == 0 else 0, 2):
                        out = bank[6 + t % 2][HD * (hh % 2):HD * (hh % 2) + HD, (hh // 2) * P:(hh // 2 + 1) * P]
                        at = (hh % 2) * 256 + c * P
                        ins = mm(out, v2[:, t - 1 + c, kv * HD:(kv + 1) * HD], pt2[:, hh // 2, at:at + P],
                                 start=c == (1 if t == 0 else 0), stop=c == 1)
                ins.then_inc(b_av, 1)
            for b in range(CB):
                pe.wait_ge(ln_sq, b + 1)
                ins = mm(bank[1][:], ones[:], ln_squares[:, 2 * b:2 * b + 2, :].rearrange("p a n -> p (a n)"),
                         start=b == 0, stop=b == CB - 1)
            ins.then_inc(ln_var, 1)
            pe.wait_ge(w_split, PW2 + 1)
            pe.wait_ge(ln_r, 1)
            for k in range(CB):
                pe.wait_ge(z_ready, k + 1)
                for m in range(4):
                    ins = products(bank[m][:], weights(PW2, k * C2 + m * P), x_hi[:, k, :], x_lo[:, k, :],
                                   k == 0, k == CB - 1)
                    if k == CB - 1:
                        ins.then_inc(pw_done if m < 3 else unit_done, 1)
            projection(5, OUT2, EV_FFN_C, [24, 24, 24, 24])
            ffn(5, FFN_C, EV_FFN_C)
            down(6, DOWN_C, EV_FFN_C + FC, 2 * FC)


def columns_unit(w, cols):
    k = w.shape[0] // P
    return w[:, cols].reshape(k, P, len(cols)).transpose(1, 0, 2).reshape(P, -1)


def rows_units(w):
    k = w.shape[0] // (2 * P)
    return list(w.reshape(k, 2, P, w.shape[1]).transpose(0, 2, 1, 3).reshape(k, P, UNIT))


def weight_units(a):
    r256 = np.arange(256)
    units = []
    w = a["conv_w_in"][0]
    for g in range(4):
        for base in (D, 2 * D, 0):
            units.append(columns_unit(w, base + 256 * g + r256))
    units += rows_units(a["conv_w_out"][0])

    def ffn(gate, up, down):
        for g in range(FC // 2):
            units.append(columns_unit(gate, 256 * g + r256))
            units.append(columns_unit(up, 256 * g + r256))
        units.extend(rows_units(down))

    gu = a["ffn_w_gate_up"]
    ffn(gu[0][:, :D_FF], gu[0][:, D_FF:], a["ffn_w_down"][0])
    halves = np.concatenate([np.arange(32) + HD * j + HALF * n for n in range(2) for j in range(4)])
    q_width = 3 * D
    for hg in range(4):
        for br in range(3):
            base = br * D + 256 * hg
            units.append(columns_unit(a["w_q"][0], base + halves))
            units.append(columns_unit(a["w_kv"], base + halves))
        for br in range(2):
            units.append(columns_unit(a["w_kv"], q_width + br * D + 256 * hg + r256))
        last = columns_unit(a["w_kv"], q_width + 2 * D + 256 * hg + r256)
        for half in np.split(last, 2, axis=1):
            units.append(np.pad(half, ((0, 0), (0, UNIT // 2))))
    units += rows_units(a["w_o"][0])
    ffn(gu[1][:, :D_FF], gu[1][:, D_FF:], a["ffn_w_down"][1])
    w = a["w_in_2"]
    for g in range(2):
        units.append(columns_unit(w, 768 + 256 * g + r256))
        units.append(columns_unit(w, 768 + C2 + 256 * g + r256))
    r64 = np.arange(HD)
    for g in range(2):
        heads = (2 * g, 2 * g + 4, 2 * g + 1, 2 * g + 5)
        units.append(columns_unit(w, np.concatenate([HD * x + r64 for x in heads])))
    units.append(columns_unit(w, 512 + r256))
    units.append(columns_unit(a["w_conv_pw_2"], np.arange(C2)))
    units += rows_units(a["w_out_2"])
    ffn(a["w_gate_2"], a["w_up_2"], a["w_down_2"])
    assert len(units) == UNITS
    return np.stack(units)


def constants():
    q, k = np.arange(P)[:, None], np.arange(P)[None, :]
    no = np.float32(NEG)
    prev = np.where(k >= q, 0, no)
    causal = np.where(k <= q, 0, no)
    residue = np.where((k <= q) & (k % 4 == q % 4), 0, no)
    masks = np.concatenate([prev, causal, residue], 1).astype(np.float32)
    ident = np.eye(P, dtype=np.float32)
    zr = (np.arange(P + 3)[None, :] == 4 * (q % 32) + 3).astype(np.float32)
    onehot = np.zeros((33, 384), np.float32)
    for x in range(384):
        dist = 255 - x
        if 0 <= dist < 128:
            bucket = dist if dist < 16 else min(31, 16 + int(math.log(dist / 16) / math.log(8) * 16))
            onehot[bucket, x] = 1
        else:
            onehot[32, x] = no
    inv_freq = (np.float32(10000.0) ** (-np.arange(HALF, dtype=np.float32) / HALF)).astype(np.float32)
    return masks, ident, zr, onehot, np.tile(inv_freq, 4)[:, None]


def kernel(**inputs):
    import concourse.bacc as bacc
    from concourse.bass_utils import run_bass_kernel_spmd

    a = {n: np.asarray(x) for n, x in inputs.items()}
    masks, ident, zr, onehot, inv_freq = constants()

    def cols(x):
        return np.asarray(x).reshape(-1, P).T

    par = np.concatenate(
        [cols(a[n]) for n in ("mix_norm_pre", "mix_norm_post", "ffn_norm_pre", "ffn_norm_post", "kv_norm",
                              "mix_pre_g_2", "mix_post_g_2", "ffn_pre_g_2", "ffn_post_g_2")]
        + [cols(a["conv_w"][0]), inv_freq], 1)
    par2 = np.concatenate([cols(a["conv_dw_2"]), cols(a["conv_dw_b_2"]), cols(a["conv_ln_g_2"]),
                           cols(a["conv_ln_b_2"]), np.tile(a["attn_sinks_2"][None, :], (P, 1))], 1)
    arrays = {
        "x_t": np.ascontiguousarray(a["x"][0].T.reshape(KC, P, S)),
        "pos": a["positions"],
        "w_all": weight_units(a),
        "par": np.ascontiguousarray(par),
        "par2": np.ascontiguousarray(par2),
        "masks": masks,
        "ident_c": ident,
        "zr_c": zr,
        "rel": np.concatenate([a["rel_bias_2"], np.ones((1, 8), np.float32)]),
        "onehot": onehot,
    }
    nc = bacc.Bacc("TRN2", target_bir_lowering=False, num_devices=1)
    aps = {n: nc.dram_tensor(n, x.shape, mybir.dt.from_np(x.dtype), kind="ExternalInput").ap()
           for n, x in arrays.items()}
    skew = nc.dram_tensor("skew", (8, P, 384), F32, kind="Internal").ap()
    out_t = nc.dram_tensor("out_t", (KC, P, S), F32, kind="ExternalOutput").ap()
    program(nc, skew=skew, out_t=out_t, **aps)
    r = run_bass_kernel_spmd(nc, [arrays], core_ids=[0])
    return np.ascontiguousarray(np.asarray(r.results[0]["out_t"]).reshape(D, S).T)[None]
```
